# Optimizing a Trainium2 kernel written in Bass

```python
import jax, jax.numpy as jnp
from jax import lax
import numpy as np

D_MODEL = 1024
BATCH = 1
SEQ = 512
DEPTH = 2
DEC_BATCH = 8
DEC_SEQ = 8
PAST_LEN = 1024
PAGE_SIZE = 128

HEAD_DIM = 64
C_A = D_MODEL // 2
H_B = (D_MODEL // 2) // HEAD_DIM
C_B = H_B * HEAD_DIM
CONV_W = 31
H_C = D_MODEL // HEAD_DIM
KV_C = H_C // 4
H_IDX = 8
D_IDX = 64
TOPK_MAX = 256
Q_BLOCK = 128
N_GROUPS = 4
E_PER_GROUP = 4
N_EXPERTS = N_GROUPS * E_PER_GROUP
D_FF_E = D_MODEL // 2
TOP_K_INNER = 2
ROPE_THETA = 10000.0
RMS_EPS = 1e-6
LN_EPS = 1e-5
N_EVEN = (DEPTH + 1) // 2
N_ODD = DEPTH // 2
IN_EVEN = 2 * C_A + 3 * C_B + H_B
IN_ODD = H_C * HEAD_DIM + 2 * KV_C * HEAD_DIM + H_IDX * D_IDX + D_IDX + H_IDX

kernel_name = 'hybrid_conv_fox_dsa_hmoe_step'

def rms_norm(x, g):
    xf = x.astype(jnp.float32)
    y = xf * lax.rsqrt(jnp.mean(xf * xf, axis=-1, keepdims=True) + RMS_EPS)
    return (y * g.astype(jnp.float32)).astype(x.dtype)

def rope(x, pos):
    half = x.shape[-1] // 2
    inv = ROPE_THETA ** (-jnp.arange(half, dtype=jnp.float32) / half)
    ang = pos.astype(jnp.float32)[:, None] * inv[None, :]
    cos = jnp.cos(ang)[None, :, None, :]
    sin = jnp.sin(ang)[None, :, None, :]
    xf = x.astype(jnp.float32)
    x1, x2 = xf[..., :half], xf[..., half:]
    return jnp.concatenate([x1 * cos - x2 * sin, x2 * cos + x1 * sin], axis=-1).astype(x.dtype)

def _query_blocks(tq):
    qb = min(Q_BLOCK, tq)
    return qb, -(-tq // qb)

def _to_blocks(a, qb, nb):
    pad = nb * qb - a.shape[1]
    a = jnp.pad(a, [(0, 0), (0, pad)] + [(0, 0)] * (a.ndim - 2), mode='edge')
    a = a.reshape((a.shape[0], nb, qb) + a.shape[2:])
    return jnp.moveaxis(a, 1, 0)

def _pos_blocks(pos, qb, nb):
    return jnp.pad(pos, (0, nb * qb - pos.shape[0]), mode='edge').reshape(nb, qb)

def _from_blocks(o, tq):
    o = jnp.moveaxis(o, 0, 1)
    o = o.reshape((o.shape[0], o.shape[1] * o.shape[2]) + o.shape[3:])
    return o[:, :tq]

def fox_attention(q, k, v, c_q, c_k, pos_q, pos_k):
    tq = q.shape[1]
    qb, nb = _query_blocks(tq)
    ck_t = jnp.swapaxes(c_k, 1, 2)
    scale = q.shape[-1] ** -0.5

    def block(args):
        q_blk, cq_blk, pq_blk = args
        s = jnp.einsum('nqhd,nkhd->nhqk', q_blk, k, preferred_element_type=jnp.float32) * scale
        s = s + jnp.swapaxes(cq_blk, 1, 2)[..., None] - ck_t[:, :, None, :]
        s = jnp.where(pos_k[None, :] <= pq_blk[:, None], s, -jnp.inf)
        p = jax.nn.softmax(s, axis=-1)
        return jnp.einsum('nhqk,nkhd->nqhd', p.astype(v.dtype), v)

    out = lax.map(block, (_to_blocks(q, qb, nb), _to_blocks(c_q, qb, nb), _pos_blocks(pos_q, qb, nb)))
    return _from_blocks(out, tq)

def dsa_attention(q, k, v, q_idx, k_idx, w_idx, pos_q, pos_k):
    n, tq, _, d = q.shape
    n_sel = min(TOPK_MAX, k.shape[1] // 4)
    qb, nb = _query_blocks(tq)
    scale = d ** -0.5
    idx_scale = D_IDX ** -0.5

    def block(args):
        q_blk, qi_blk, wi_blk, pq_blk = args
        dots = jnp.einsum('nqhe,nke->nqhk', qi_blk, k_idx, preferred_element_type=jnp.float32) * idx_scale
        score = jnp.einsum('nqhk,nqh->nqk', jax.nn.relu(dots), wi_blk.astype(jnp.float32))
        score = jnp.where((pos_k[None, :] <= pq_blk[:, None])[None], score, -jnp.inf)
        _, sel = lax.top_k(score, n_sel)
        valid = pos_k[sel] <= pq_blk[None, :, None]
        k_sel = jax.vmap(lambda kk, ii: kk[ii])(k, sel)
        v_sel = jax.vmap(lambda vv, ii: vv[ii])(v, sel)
        qg = q_blk.reshape(n, qb, KV_C, H_C // KV_C, d)
        s = jnp.einsum('nqgrd,nqkgd->nqgrk', qg, k_sel, preferred_element_type=jnp.float32) * scale
        s = jnp.where(valid[:, :, None, None, :], s, -jnp.inf)
        p = jax.nn.softmax(s, axis=-1)
        o = jnp.einsum('nqgrk,nqkgd->nqgrd', p.astype(v.dtype), v_sel)
        return o.reshape(n, qb, H_C, d)

    out = lax.map(block, (_to_blocks(q, qb, nb), _to_blocks(q_idx, qb, nb),
                          _to_blocks(w_idx, qb, nb), _pos_blocks(pos_q, qb, nb)))
    return _from_blocks(out, tq)

def even_mixer(h, conv_state, past_k, past_v, past_logf, w_in, b_forget, w_dw, b_dw, ln_g, ln_b, w_out):
    n, t, _ = h.shape
    p = past_k.shape[1]
    proj = jnp.einsum('ntd,de->nte', h, w_in)
    a_val, a_gate, q, k, v, f_logit = jnp.split(
        proj, [C_A, 2 * C_A, 2 * C_A + C_B, 2 * C_A + 2 * C_B, 2 * C_A + 3 * C_B], axis=-1)
    u = a_val * jax.nn.sigmoid(a_gate)
    buf = jnp.concatenate([conv_state.astype(u.dtype), u], axis=1)
    conv = lax.conv_general_dilated(buf, w_dw.astype(u.dtype)[:, None, :], (1,), 'VALID',
                                    dimension_numbers=('NWC', 'WIO', 'NWC'),
                                    feature_group_count=C_A) + b_dw
    cf = conv.astype(jnp.float32)
    mu = jnp.mean(cf, axis=-1, keepdims=True)
    var = jnp.mean(jnp.square(cf - mu), axis=-1, keepdims=True)
    cn = (cf - mu) * lax.rsqrt(var + LN_EPS) * ln_g.astype(jnp.float32) + ln_b.astype(jnp.float32)
    a_out = jax.nn.silu(cn).astype(h.dtype)
    new_conv = buf[:, -(CONV_W - 1):]
    q = q.reshape(n, t, H_B, HEAD_DIM)
    k = k.reshape(n, t, H_B, HEAD_DIM)
    v = v.reshape(n, t, H_B, HEAD_DIM)
    logf = jax.nn.log_sigmoid(f_logit.astype(jnp.float32) + b_forget.astype(jnp.float32))
    k_all = jnp.concatenate([past_k.astype(k.dtype), k], axis=1)
    v_all = jnp.concatenate([past_v.astype(v.dtype), v], axis=1)
    c_all = jnp.cumsum(jnp.concatenate([past_logf.astype(jnp.float32), logf], axis=1), axis=1)
    pos_k = jnp.arange(p + t)
    pos_q = p + jnp.arange(t)
    b_out = fox_attention(q, k_all, v_all, c_all[:, p:], c_all, pos_q, pos_k)
    mixed = jnp.concatenate([a_out, b_out.reshape(n, t, C_B).astype(h.dtype)], axis=-1)
    return jnp.einsum('nte,ed->ntd', mixed, w_out), new_conv, k, v, logf

def odd_mixer(h, past_k, past_v, past_kidx, w_in, w_out):
    n, t, _ = h.shape
    p = past_k.shape[1]
    s1 = H_C * HEAD_DIM
    s2 = s1 + KV_C * HEAD_DIM
    s3 = s2 + KV_C * HEAD_DIM
    s4 = s3 + H_IDX * D_IDX
    s5 = s4 + D_IDX
    proj = jnp.einsum('ntd,de->nte', h, w_in)
    q, k, v, qi, ki, wi = jnp.split(proj, [s1, s2, s3, s4, s5], axis=-1)
    pos_q = p + jnp.arange(t)
    q = rope(q.reshape(n, t, H_C, HEAD_DIM), pos_q)
    k = rope(k.reshape(n, t, KV_C, HEAD_DIM), pos_q)
    v = v.reshape(n, t, KV_C, HEAD_DIM)
    qi = rope(qi.reshape(n, t, H_IDX, D_IDX), pos_q)
    ki = rope(ki[:, :, None, :], pos_q)[:, :, 0]
    k_all = jnp.concatenate([past_k.astype(k.dtype), k], axis=1)
    v_all = jnp.concatenate([past_v.astype(v.dtype), v], axis=1)
    ki_all = jnp.concatenate([past_kidx.astype(ki.dtype), ki], axis=1)
    pos_k = jnp.arange(p + t)
    o = dsa_attention(q, k_all, v_all, qi, ki_all, wi * (H_IDX ** -0.5), pos_q, pos_k)
    return jnp.einsum('nte,ed->ntd', o.reshape(n, t, H_C * HEAD_DIM), w_out), k, v, ki

def hier_moe(h, w_group, b_group, w_router, b_router, w_gate, w_up, w_down):
    n, t, d = h.shape
    m = n * t
    x2 = h.reshape(m, d)
    g_logits = jnp.einsum('md,dg->mg', x2, w_group, preferred_element_type=jnp.float32) + b_group.astype(jnp.float32)
    g_w, g_idx = lax.top_k(jax.nn.softmax(g_logits, axis=-1), 1)
    e_logits = (jnp.einsum('md,de->me', x2, w_router, preferred_element_type=jnp.float32)
                + b_router.astype(jnp.float32)).reshape(m, N_GROUPS, E_PER_GROUP)
    e_in = e_logits[jnp.arange(m), g_idx[:, 0]]
    top_v, top_i = lax.top_k(e_in, TOP_K_INNER)
    top_w = jax.nn.softmax(top_v, axis=-1) * g_w
    expert_id = g_idx * E_PER_GROUP + top_i
    combine = jnp.einsum('mk,mke->me', top_w, jax.nn.one_hot(expert_id, N_EXPERTS, dtype=jnp.float32))
    y = jnp.zeros((m, d), jnp.float32)
    for e in range(N_EXPERTS):
        hid = jax.nn.silu(x2 @ w_gate[e]) * (x2 @ w_up[e])
        y = y + combine[:, e:e + 1] * (hid @ w_down[e]).astype(jnp.float32)
    return y.astype(h.dtype).reshape(n, t, d)

def setup_inputs(seed: int = 0) -> dict:
    key = jax.random.key(seed)
    keys = jax.random.split(key, 48)
    counter = [0]

    def nxt():
        counter[0] += 1
        return keys[counter[0] - 1]

    def nrm(shape, scale=1.0):
        return jax.random.normal(nxt(), shape, jnp.float32) * scale

    n_pages = PAST_LEN // PAGE_SIZE
    n_used = DEC_BATCH * n_pages
    n_pool = n_used + max(1, n_used // 4)
    inp = {}
    inp['x_prompt'] = nrm((BATCH, SEQ, D_MODEL))
    inp['x_sample'] = nrm((DEC_BATCH, DEC_SEQ, D_MODEL))
    inp['state_conv'] = nrm((N_EVEN, DEC_BATCH, CONV_W - 1, C_A), 0.5)
    inp['cache_fox_k'] = nrm((N_EVEN, n_pool, PAGE_SIZE, H_B, HEAD_DIM))
    inp['cache_fox_v'] = nrm((N_EVEN, n_pool, PAGE_SIZE, H_B, HEAD_DIM))
    inp['cache_fox_logf'] = jax.nn.log_sigmoid(4.0 + nrm((N_EVEN, n_pool, PAGE_SIZE, H_B)))
    inp['cache_dsa_k'] = nrm((N_ODD, n_pool, PAGE_SIZE, KV_C, HEAD_DIM))
    inp['cache_dsa_v'] = nrm((N_ODD, n_pool, PAGE_SIZE, KV_C, HEAD_DIM))
    inp['cache_dsa_kidx'] = nrm((N_ODD, n_pool, PAGE_SIZE, D_IDX))
    inp['page_table'] = jax.random.permutation(nxt(), n_pool)[:n_used].reshape(DEC_BATCH, n_pages).astype(jnp.int32)
    inp['norm_mix_even'] = 1.0 + nrm((N_EVEN, D_MODEL), 0.02)
    inp['w_in_even'] = nrm((N_EVEN, D_MODEL, IN_EVEN), D_MODEL ** -0.5)
    inp['b_forget'] = jax.random.uniform(nxt(), (N_EVEN, H_B), jnp.float32, minval=2.0, maxval=6.0)
    inp['w_dw'] = nrm((N_EVEN, CONV_W, C_A), CONV_W ** -0.5)
    inp['b_dw'] = nrm((N_EVEN, C_A), 0.01)
    inp['ln_conv_g'] = 1.0 + nrm((N_EVEN, C_A), 0.02)
    inp['ln_conv_b'] = nrm((N_EVEN, C_A), 0.01)
    inp['w_out_even'] = nrm((N_EVEN, C_A + C_B, D_MODEL), (C_A + C_B) ** -0.5)
    inp['norm_mix_odd'] = 1.0 + nrm((N_ODD, D_MODEL), 0.02)
    inp['w_in_odd'] = nrm((N_ODD, D_MODEL, IN_ODD), D_MODEL ** -0.5)
    inp['w_out_odd'] = nrm((N_ODD, H_C * HEAD_DIM, D_MODEL), (H_C * HEAD_DIM) ** -0.5)
    inp['norm_ffn'] = 1.0 + nrm((DEPTH, D_MODEL), 0.02)
    inp['w_group'] = nrm((DEPTH, D_MODEL, N_GROUPS), D_MODEL ** -0.5)
    inp['b_group'] = nrm((DEPTH, N_GROUPS), 0.01)
    inp['w_router'] = nrm((DEPTH, D_MODEL, N_EXPERTS), D_MODEL ** -0.5)
    inp['b_router'] = nrm((DEPTH, N_EXPERTS), 0.01)
    inp['w_gate'] = nrm((DEPTH, N_EXPERTS, D_MODEL, D_FF_E), D_MODEL ** -0.5)
    inp['w_up'] = nrm((DEPTH, N_EXPERTS, D_MODEL, D_FF_E), D_MODEL ** -0.5)
    inp['w_down'] = nrm((DEPTH, N_EXPERTS, D_FF_E, D_MODEL), D_FF_E ** -0.5)
    inp['norm_final'] = 1.0 + nrm((D_MODEL,), 0.02)
    return inp

def reference(x_prompt, x_sample, state_conv, cache_fox_k, cache_fox_v, cache_fox_logf,
              cache_dsa_k, cache_dsa_v, cache_dsa_kidx, page_table,
              norm_mix_even, w_in_even, b_forget, w_dw, b_dw, ln_conv_g, ln_conv_b, w_out_even,
              norm_mix_odd, w_in_odd, w_out_odd,
              norm_ffn, w_group, b_group, w_router, b_router, w_gate, w_up, w_down, norm_final):
    n_p = x_prompt.shape[0]
    n_s = x_sample.shape[0]
    dt_p = x_prompt.dtype

    def paged_rows(pool):
        rows = pool[page_table]
        return rows.reshape((n_s, rows.shape[1] * rows.shape[2]) + rows.shape[3:])

    hp, hs = x_prompt, x_sample
    conv_p, conv_s, fk_p, fk_s, fv_p, fv_s, fl_p, fl_s = [], [], [], [], [], [], [], []
    dk_p, dk_s, dv_p, dv_s, di_p, di_s = [], [], [], [], [], []
    for layer in range(DEPTH):
        i = layer // 2
        if layer % 2 == 0:
            w = (w_in_even[i], b_forget[i], w_dw[i], b_dw[i], ln_conv_g[i], ln_conv_b[i], w_out_even[i])
            yp, cp, kp, vp, lp = even_mixer(
                rms_norm(hp, norm_mix_even[i]), jnp.zeros((n_p, CONV_W - 1, C_A), dt_p),
                jnp.zeros((n_p, 0, H_B, HEAD_DIM), dt_p), jnp.zeros((n_p, 0, H_B, HEAD_DIM), dt_p),
                jnp.zeros((n_p, 0, H_B), jnp.float32), *w)
            ys, cs, ks, vs, ls = even_mixer(
                rms_norm(hs, norm_mix_even[i]), state_conv[i], paged_rows(cache_fox_k[i]),
                paged_rows(cache_fox_v[i]), paged_rows(cache_fox_logf[i]), *w)
            conv_p.append(cp); conv_s.append(cs)
            fk_p.append(kp); fk_s.append(ks)
            fv_p.append(vp); fv_s.append(vs)
            fl_p.append(lp); fl_s.append(ls)
        else:
            yp, kp, vp, ip = odd_mixer(
                rms_norm(hp, norm_mix_odd[i]), jnp.zeros((n_p, 0, KV_C, HEAD_DIM), dt_p),
                jnp.zeros((n_p, 0, KV_C, HEAD_DIM), dt_p), jnp.zeros((n_p, 0, D_IDX), dt_p),
                w_in_odd[i], w_out_odd[i])
            ys, ks, vs, is_ = odd_mixer(
                rms_norm(hs, norm_mix_odd[i]), paged_rows(cache_dsa_k[i]), paged_rows(cache_dsa_v[i]),
                paged_rows(cache_dsa_kidx[i]), w_in_odd[i], w_out_odd[i])
            dk_p.append(kp); dk_s.append(ks)
            dv_p.append(vp); dv_s.append(vs)
            di_p.append(ip); di_s.append(is_)
        hp = hp + yp
        hs = hs + ys
        moe_w = (w_group[layer], b_group[layer], w_router[layer], b_router[layer],
                 w_gate[layer], w_up[layer], w_down[layer])
        hp = hp + hier_moe(rms_norm(hp, norm_ffn[layer]), *moe_w)
        hs = hs + hier_moe(rms_norm(hs, norm_ffn[layer]), *moe_w)
    y_prompt = rms_norm(hp, norm_final)
    y_sample = rms_norm(hs, norm_final)
    conv_state_prompt = jnp.stack(conv_p)
    conv_state_sample = jnp.stack(conv_s)
    fox_k_prompt = jnp.stack(fk_p)
    fox_k_sample = jnp.stack(fk_s)
    fox_v_prompt = jnp.stack(fv_p)
    fox_v_sample = jnp.stack(fv_s)
    fox_logf_prompt = jnp.stack(fl_p)
    fox_logf_sample = jnp.stack(fl_s)
    dsa_k_prompt = jnp.stack(dk_p)
    dsa_k_sample = jnp.stack(dk_s)
    dsa_v_prompt = jnp.stack(dv_p)
    dsa_v_sample = jnp.stack(dv_s)
    dsa_kidx_prompt = jnp.stack(di_p)
    dsa_kidx_sample = jnp.stack(di_s)
    return (y_prompt, y_sample, conv_state_prompt, conv_state_sample, fox_k_prompt, fox_k_sample,
            fox_v_prompt, fox_v_sample, fox_logf_prompt, fox_logf_sample, dsa_k_prompt, dsa_k_sample,
            dsa_v_prompt, dsa_v_sample, dsa_kidx_prompt, dsa_kidx_sample)


_drawn_inputs = setup_inputs


def setup_inputs(seed=0):
    import zlib

    import numpy as np

    out = dict(_drawn_inputs(seed))
    spreads = {}
    factors = {'ln_conv_b': 2.896, 'b_router': 3.223, 'norm_final': 2.923}
    for name, (base, spread) in spreads.items():
        noise = np.random.default_rng([zlib.crc32(name.encode()), seed]).standard_normal(out[name].shape)
        drawn = base * np.exp(spread * noise) if base else spread * noise
        out[name] = __import__('jax').numpy.asarray(drawn.astype(out[name].dtype))
    for name, factor in factors.items():
        out[name] = (out[name] * factor).astype(out[name].dtype)
    return out
```

```python
from contextlib import ExitStack

import numpy as np
import concourse.bass as bass
from concourse import mybir

F32 = mybir.dt.float32
F16 = mybir.dt.float16
U32 = mybir.dt.uint32
I32 = mybir.dt.int32
ALU = mybir.AluOpType
ACT = mybir.ActivationFunctionType
X = mybir.AxisListType.X

D = 1024
SEQ = 512
NS = 8
DS = 8
NSAMP = NS * DS
TOK = SEQ + NSAMP
NT = 5
PAST = 1024
PAGE = 128
NPG = PAST // PAGE
HB = 8
HC = 16
KVC = 4
HI = 8
CW = 31
CA = 512
NE = 16
NG = 4
FF = 512
DC = D // 128
LK = PAST + DS
CAP = 128
ROWS = 640
NEG = -1e30
LAST = 16384.0
TAKEN = -3e38
TOPP = min(256, SEQ // 4)
TOPS = min(256, LK // 4)
NBLK = (5, 4)
TAIL = (8, 72)
RING = 3
U_TURNS = {10: (0, 1), 11: (2, 3), 12: (4,)}
S_BANK = (0, 1, 6)


SPILLS = (TOK * 2 - 1) // CAP

OPEN = 1
STEPS = {}
_at = OPEN
for _n, _w in (("places", 1), ("token_mm", 1), ("token", 1), ("token_seen", 1), ("turned", 1), ("inputs", 1),
               ("gate_up", 1), ("silu", 1), ("hid", 1), ("hid_turned", 1), ("hidt", 1), ("down", 1), ("copied", 1),
               ("stored", 16), ("stored_seen", 1)):
    _at += _w
    STEPS[_n] = _at
TURN = _at - OPEN


def rows(t):
    return 128 if t < 4 else NSAMP


REGIONS = {}
_at = 0
for _n, _w in (("H", NT * D), ("XT", DC * TOK), ("RING", RING * 4096), ("CR", 8192), ("A3", NT * 512),
               ("QT", 8 * TOK), ("X", 8640), ("WORK", 5120), ("IDENT", 128), ("SMALL", 168), ("ROPE", 320),
               ("CAUS", 512), ("ROUT", 320), ("ONES", 128), ("MISC", 480)):
    REGIONS[_n] = _at
    _at += _w
ARENA = _at


SHARED = (
    (NE, "gate_mm up_mm down_mm silu hid hid_turned hidt y_a y_v xgt xg_used idx"),
    (10, "out_mm out_add"),
    (NT, "hn hn_t xt sq combined dmat tok_mm"),
    (1, "ms root route_mm mask pos_mm tok turns row_u tail_mm qbd"),
    (2, "tail_ev route_dve route_act"),
    (5 * NBLK[0], "proj_mm proj_ev"),
    (4 * HB, "s_mm sb nmx exp probs p_turned pt_ev"),
    (HB, "pv o_ev"),
    (NS, "scored exp_s nmx_s pv_s o_turned os_ev osum"),
    (3 * NS, "ps_turned pts_ev"),
    (15, "turned turn_ev"),
    (64, "vnew"),
    (128, "xg y_rows"),
)
PER = {stem: n for n, stems in SHARED for stem in stems.split()}
PER_PARITY = {"hn_out": (48, 32), "yb": (48, 48, 32, 32)}


def first_block(layer, part):
    at = 0
    for l in range(2):
        for p, n in (("in", NBLK[l]), ("out", 2), ("moe", 3 * NE)):
            if (l, p) == (layer, part):
                return at
            at += n
    return at


def trunk(nc, a, o):
    ctx = ExitStack()
    arena = ctx.enter_context(nc.sbuf_tensor("arena", [128, ARENA], F32))
    psum = ctx.enter_context(nc.psum_tensor("banks", [128, 4096], F32))
    sems = {}

    def split(name):
        stem = name.rstrip("0123456789_")
        n = name[len(stem):].split("_")
        if stem in PER:
            return "_".join([stem] + n[1:]), int(n[0]) * PER[stem]
        if stem in PER_PARITY:
            return "_".join([stem] + n[1:]), int(n[0]) * PER_PARITY[stem][int(n[1])]
        return name, 0

    def S(name):
        name = split(name)[0]
        if name not in sems:
            sems[name] = ctx.enter_context(nc.semaphore(name))
        return sems[name]

    def upto(name, value):
        return value + split(name)[1]

    def past(value):
        return not isinstance(value, int) or value > 0

    def at(region, off, width, p0=0, p1=128):
        c = REGIONS[region] + off
        return arena[p0:p1, c:c + width]

    def bank(b, c0=0, c1=512, p0=0, p1=128):
        return psum[p0:p1, 512 * b + c0:512 * b + c1]

    def g3(ap, n):
        return ap.rearrange("p (n w) -> p n w", n=n)

    def bc_last(ap, n):
        return ap.unsqueeze(len(ap.shape)).broadcast_to(list(ap.shape) + [n])

    def bc_mid(ap, n):
        return ap.unsqueeze(1).broadcast_to([ap.shape[0], n] + list(ap.shape[1:]))

    h = g3(at("H", 0, NT * D), NT)
    xt = g3(at("XT", 0, DC * TOK), DC)
    ring = [at("RING", 4096 * i, 4096) for i in range(RING)]
    ident = at("IDENT", 0, 128)
    gain = [at("SMALL", 8 * i, 8) for i in range(4)]
    bdw = at("SMALL", 32, 4)
    lng = at("SMALL", 36, 4)
    lnb = at("SMALL", 40, 4)
    wdw = g3(at("SMALL", 44, 124), 4)
    rope = g3(at("ROPE", 0, 320), NT)
    causal = at("CAUS", 0, 512)
    wrout = [g3(at("ROUT", 160 * i, 160), DC) for i in range(2)]
    mean_m = at("ONES", 0, 128)
    k_new_odd = g3(at("ONES", 0, 128), 2)
    before16 = at("MISC", 0, 64).bitcast(F16)
    ones16 = at("MISC", 64, 64).bitcast(F16)
    slot16 = at("MISC", 128, 64).bitcast(F16)
    tokid16 = at("MISC", 192, 3).bitcast(F16)
    bvec = at("MISC", 196, 48)
    ssq = at("MISC", 244, 5)
    rstd = at("MISC", 250, 5)
    mx = at("MISC", 460, 3)
    nmx = at("MISC", 464, 3)
    esum = at("MISC", 256, 3)
    rsum = at("MISC", 260, 3)
    idxc = [at("MISC", 266 + i, 1).bitcast(U32) for i in range(2)]
    lft = g3(at("MISC", 268, 40), NT)
    max8 = at("MISC", 308, 8)
    wis = g3(at("MISC", 316, 40), NT)
    wcol = at("MISC", 356, 8, 0, 64)
    new_mask = at("MISC", 364, 8, 0, 64)
    pages = at("MISC", 372, NS * NPG, 0, 1).bitcast(I32)

    spill_base = at("MISC", 444, 8)
    spill_used = at("MISC", 452, 8, 0, 1).bitcast(I32)
    spill_block = at("MISC", 468, 8, 0, 1).bitcast(I32)
    tick = [at("MISC", 440 + i, 1, 0, 1) for i in range(3)]

    A0 = g3(at("CR", 0, NT * 1024), NT)
    conv_p = A0[:, 0:4, 512:1024]
    conv_s = g3(A0[:, 4, 512:768], 4)
    A1 = g3(at("CR", NT * 1024, NT * 512), NT)
    A2 = g3(at("WORK", 0, NT * 512), NT)
    A3 = g3(at("A3", 0, NT * 512), NT)
    tail_odd = g3(at("CR", 7680, NT * 72), NT)
    qt = g3(at("QT", 0, 8 * TOK), 8)
    ucp = g3(at("X", 0, 2168), 4)
    ucs = g3(at("X", 2168, 1216), 4)
    tri = at("X", 3384, 1032)
    self_ = g3(at("X", 4416, 512, 0, 72), NS)
    cks = at("X", 4928, 1032)
    ckp = at("X", 5960, 512, 0, 8)
    qbd_even = at("X", 6472, 2048).rearrange("p (c s r) -> p c s r", c=4, s=NS)
    kd = g3(at("X", 0, 2304), 4)
    qi = g3(at("X", 2304, 2304), 4)
    ki = at("X", 4608, 576)
    selp = [at("X", 5184 + 64 * t * (t + 1), 128 * (t + 1)) for t in range(4)]
    sels = at("X", 6464, 1032, 0, 64)
    es = g3(at("X", 7496, 1024, 0, 64), NS)
    ohw = at("X", 8520, 120, 0, 64)
    qbd_odd = at("X", 2304, 2048).rearrange("p (c s r) -> p c s r", c=2, s=NS)
    sb = [[at("WORK", 0, 512), at("WORK", 512, 512), at("X", off, 512)] for off in (0, 4608)]
    pt = [g3(at("WORK", 1024 + 2048 * i, 2048), 4) for i in range(2)]
    prs = [at("WORK", 1032 * i, 1032) for i in range(2)]
    pts = [at("WORK", 2064 + 1152 * i, 1152) for i in range(2)]
    k_even = [at("CR", 0, 4096), ring[0]]
    kv_odd = [at("CR", 0, 4096), at("CR", 4096, 4096), ring[first_block(1, "moe") % RING]]
    v_even = [at("CR", 4096, 4096), ring[1]]
    o_s = at("WORK", 4368, 64)
    o2 = at("WORK", 4432, 128)
    zeros = at("A3", 0, 1024)
    tap = [at("WORK", 2560 + 256 * i, 256) for i in range(2)]
    vnew = [[at("A3", 512 * i, 512, 0, 8) for i in range(2)],
            [at("A3", 512 * i, 256, 0, 8) for i in range(2)]]
    t1 = at("A3", 1024, 512)
    headmask = at("A3", 1536, 512, 0, 64)
    hn = [at("WORK", 1024 * i, 1024) for i in range(2)]
    junk = at("WORK", 2048, 1024)
    wtail = [g3(at("WORK", 3072, 8 * w), DC) for w in TAIL]
    dmat = [g3(at("WORK", 2048 + 1024 * i, 1024).bitcast(F16), NE) for i in range(2)]

    places = [g3(at("WORK", 2048 + 320 * i, 320).bitcast(F16), NT) for i in range(2)]

    def rt_buf(off, width):
        return at("WORK", 4096 + off, width)
    over_w = [at("CR", 4096 * i, 4096) for i in range(3)]
    xg = [at("X", 1024 * i, 1024) for i in range(2)]
    xgt = [g3(at("X", 2048 + 1024 * i, 1024), DC) for i in range(2)]
    yout = [at("X", 4096 + 1024 * i, 1024) for i in range(2)]
    sil = at("X", 6144, 512)
    hid = at("X", 6656, 512)
    hidt = g3(at("X", 7168, 512), 4)
    ybuf = [at("X", 1024 * i, 1024) for i in range(4)]
    lfa = g3(at("WORK", 3648, 512), NPG)
    nlf = at("WORK", 4160, 64, 0, 8)
    fin_g = at("CR", 0, 1024)
    yfin = [at("CR", 1024 + 1024 * i, 1024) for i in range(2)]

    tok_u = rt_buf(0, NE).bitcast(U32)
    row_u = rt_buf(16, 2 * NT).bitcast(U32)
    mask16 = g3(rt_buf(26, 40).bitcast(F16), NT)
    logits = g3(rt_buf(66, 100), NT)
    wts = rt_buf(166, 2 * NT)
    posm = g3(rt_buf(176, 80), NT)
    oh = [g3(rt_buf(256 + 80 * i, 80), NT) for i in range(2)]
    rtmp = [rt_buf(416 + 80 * i, 80) for i in range(4)]
    sm = [rt_buf(736 + 20 * i, 20) for i in range(8)]
    rowf = rtmp[2][:, 20:20 + 2 * NT]
    pick4 = rt_buf(900, 20)
    num16 = rt_buf(920, 16)
    sqv = g3(at("WORK", 0, 4 * TOK), 4)
    lnv = at("WORK", 2304, TOK)
    score_p = [xt[:, t, 0:128 * (t + 1)] for t in range(4)]
    relu = [at("WORK", 1280 + 512 * i, 512) for i in range(2)]
    rw = at("WORK", 2304, LK, 0, 64)
    score_s = ring[first_block(1, "moe") % RING][0:64, 0:LK]
    qis = at("WORK", 4368, 512, 0, 64)
    rot = [at("WORK", 512 * i, 512) for i in range(2)]
    kdup = [at("WORK", 1024 + 640 * i, 640) for i in range(2)]
    lf_tmp = [at("WORK", 4224 + 40 * i, 40) for i in range(3)]

    hn_d = nc.dram_tensor("hn_scratch", (TOK, D), F32, kind="Internal").ap()
    y_d = nc.dram_tensor("expert_rows", ((NE + SPILLS) * CAP, D), F32, kind="Internal").ap()
    wi_d = nc.dram_tensor("wi_scratch", (NSAMP, HI), F32, kind="Internal").ap()

    TILES = [(t, 128 * t, 128 * t + rows(t)) for t in range(NT)]

    def block_done(k):
        for l in range(2):
            i = k - first_block(l, "in")
            if 0 <= i < NBLK[l]:
                return f"proj_mm{l}", 5 * (i + 1)
            i = k - first_block(l, "out")
            if 0 <= i < 2:
                return f"out_mm{l}", 5 * (i + 1)
            i = k - first_block(l, "moe")
            if 0 <= i < 3 * NE:
                return ("gate_mm", "up_mm", "down_mm")[i % 3] + str(l), i // 3 + 1

    def h_ready(eng, n, t):
        if n == 0:
            eng.wait_ge(S("x_in"), 32)
        elif n % 2:
            eng.wait_ge(S(f"out_add{n // 2}"), upto(f"out_add{n // 2}", 5 + t + 1))
        else:
            eng.wait_ge(S(f"combined{n // 2 - 1}"), upto(f"combined{n // 2 - 1}", t + 1))

    def further_rounds(eng, body, first=0):
        with eng.If(eng.value_load(spill_used[:, 0:1], min_val=0, max_val=1) > 0):
            if first == 0:
                body(0)
            with eng.If(eng.value_load(spill_used[:, 1:2], min_val=0, max_val=1) > 0):
                with eng.Fori(1, SPILLS) as i:
                    with eng.If(eng.value_load(spill_used[:, bass.ds(i, 1)], min_val=0, max_val=1) > 0):
                        body(i)

    def page_rows(ap, page):
        return ap[bass.ds(page, 1)].rearrange("a p w -> (a p) w")

    block = ctx.enter_context(nc.Block())

    @block.sync
    def _(sp):
        def stream(k):
            if k >= RING:
                name, count = block_done(k - RING)
                sp.wait_ge(S(name), upto(name, count))
            sp.dma_start(ring[k % RING], a["wstream"][k]).then_inc(S(f"ring{k % RING}"), 16)

        sp.dma_start(h[:, 0:4, :], a["x_prompt"].rearrange("(t p) d -> p t d", p=128)).then_inc(S("x_in"), 16)
        sp.dma_start(h[0:NSAMP, 4, :], a["x_sample"]).then_inc(S("x_in"), 16)
        sp.dma_start(ident, a["ident"]).then_inc(S("c_ident"), 16)
        sp.dma_start(at("SMALL", 0, 168), a["small"]).then_inc(S("c_small"), 16)
        stream(0)
        sp.dma_start(at("WORK", 3072, 64), a["wtail0"]).then_inc(S("c_tail0"), 16)
        sp.dma_start(bvec, a["bvec"]).then_inc(S("c_misc"), 16)
        sp.dma_start(causal, a["causal"]).then_inc(S("c_misc"), 16)
        sp.dma_start(mean_m, a["mean_m"]).then_inc(S("c_misc"), 16)
        sp.dma_start(at("MISC", 0, 195), a["misc"]).then_inc(S("c_misc"), 16)
        sp.dma_start(at("ROUT", 0, 320), a["wrouter"]).then_inc(S("c_misc"), 16)
        sp.dma_start(tri, a["tri"]).then_inc(S("c_even"), 16)
        sp.dma_start(at("X", 4416, 512, 0, 72), a["selF"]).then_inc(S("c_even"), 16)
        sp.dma_start(at("X", 4928, 1032, 64, 72), a["new_rows"]).then_inc(S("c_even"), 16)
        sp.dma_start(ucs[:, :, :].rearrange("p c (s w) -> p c s w", s=NS)[:, :, :, 0:30],
                     a["conv_state_t"])\
            .then_inc(S("c_even"), 16)
        sp.dma_start(pages, a["page_table"]).then_inc(S("page_table"), 16)
        for k in range(1, 3):
            stream(k)
        sp.dma_start(at("ROPE", 0, 320), a["rope"]).then_inc(S("c_misc"), 16)
        sp.wait_ge(S("page_table"), 16)

        def page_id(s, j):
            return sp.value_load(pages[0:1, NPG * s + j:NPG * s + j + 1], min_val=0, max_val=a["n_pool"] - 1)

        for s in range(NS):
            for j in range(NPG):
                sp.dma_start(lfa[:, j, 8 * s:8 * s + 8], page_rows(a["logf"], page_id(s, j))).then_inc(S("lf_in"), 16)

        for k in range(3, first_block(0, "out") + 1):
            stream(k)
        sp.wait_ge(S("logf_out"), 32)
        sp.dma_start(nlf, o["fox_logf_sample"].rearrange("a s j h -> j (a s) h")).then_inc(S("nlf_in"), 16)

        sp.wait_ge(S("turned0"), 15)
        sp.wait_ge(S("u_out"), 16 * (1 + NS))
        sp.wait_ge(S("squares"), 1)
        for s in range(NS):
            if s == 1:
                sp.wait_ge(S("proj_mm0"), 5 * NBLK[0])
            if s >= 2:
                sp.wait_ge(S("scored0"), s - 1)
            for j in range(NPG):
                sp.dma_start(g3(k_even[s % 2], NPG)[:, j, :], page_rows(a["fox_kt"], page_id(s, j)))\
                    .then_inc(S(f"kv{s % 2}"), 16)
            if s >= 2:
                sp.wait_ge(S("pv_s0"), s - 1)
            for j in range(NPG):
                sp.dma_start(g3(v_even[s % 2], NPG)[:, j, :], page_rows(a["fox_v"], page_id(s, j)))\
                    .then_inc(S(f"kv{2 + s % 2}"), 16)
            if s == 0:
                sp.wait_ge(S("pv0"), HB)
                sp.wait_ge(S("fox_v_out"), 32)
                sp.dma_start(headmask, a["headmask"]).then_inc(S("headmask"), 16)
            if s >= 2:
                sp.wait_ge(S("pv_s0"), s - 1)
            sp.dma_start(vnew[0][s % 2],
                         o["fox_v_sample"][0, s].rearrange("j h d -> j (h d)"))\
                .then_inc(S(f"vnew0_{s % 2}"), 16)
        sp.wait_ge(S("scored0"), NS)
        stream(first_block(0, "out") + 1)
        sp.wait_ge(S("pv_s0"), NS)
        stream(first_block(0, "moe"))

        def experts(l):
            b = first_block(l, "moe")
            stream(b + 1)
            stream(b + 2)
            stream(b + 3)
            for j, (e0, e1) in enumerate(((1, 4), (4, 8), (8, 12), (12, NE - 1))):
                if j:
                    sp.wait_ge(S(f"turns{l}"), upto(f"turns{l}", 1))
                    with sp.If(sp.value_load(spill_used[:, 0:1], min_val=0, max_val=1) > 0):
                        k = sp.value_load(spill_block[:, 0:1], min_val=0, max_val=3 * NE - 3)
                        sp.dma_start(over_w[j - 1], a["wstream"][bass.ds(k + (b + j - 1), 1)].rearrange("a p w -> (a p) w"))\
                            .then_inc(S(f"general_w{l}_"), 16)
                with sp.Fori(e0, e1) as n:
                    for i in (1, 2, 3):
                        name = ("gate_mm", "up_mm", "down_mm")[i % 3] + str(l)
                        sp.wait_ge(S(name), upto(name, n + (1 if i == 3 else 0)))
                        sp.wait_ge(S("x_in"), 32)
                        sp.dma_start(ring[(b + i) % RING],
                                     a["wstream"][bass.ds(b + i + 3 * n, 1)].rearrange("a p w -> (a p) w"))\
                            .then_inc(S(f"ring{(b + i) % RING}"), 16)
            stream(b + 3 * NE - 2)
            stream(b + 3 * NE - 1)

        def spilled(l):
            b = first_block(l, "moe")

            def turn(i):
                k = sp.value_load(spill_block[:, bass.ds(i, 1)], min_val=0, max_val=3 * NE - 3)
                sp.wait_ge(S(f"general{l}_"), i * TURN + OPEN)
                sp.wait_ge(S("x_in"), 32)
                for j in range(3):
                    sp.dma_start(over_w[j],
                                 a["wstream"][bass.ds(k + (b + j), 1)].rearrange("a p w -> (a p) w"))\
                        .then_inc(S(f"general_w{l}_"), 16)

            further_rounds(sp, turn, 1)

        experts(0)
        for k in range(first_block(1, "in"), first_block(1, "in") + 3):
            stream(k)
        spilled(0)
        sp.wait_ge(S("combined0"), NT)
        sp.dma_start(at("WORK", 3072, 576), a["wtail1"]).then_inc(S("c_tail1"), 16)
        stream(first_block(1, "in") + 3)
        sp.dma_start(es[:, :, :].rearrange("p s r -> p (s r)"), a["es"]).then_inc(S("c_odd"), 16)
        sp.dma_start(ohw, a["ohw"]).then_inc(S("c_odd"), 16)
        sp.dma_start(new_mask, a["new_mask"]).then_inc(S("c_odd"), 16)
        for k in (first_block(1, "out"), first_block(1, "out") + 1):
            stream(k)
        sp.wait_ge(S("wi_out"), 16)
        for hh in range(HI):
            sp.dma_start(at("MISC", 356, 8, 8 * hh, 8 * hh + 8), wi_d[:, hh].rearrange("(s q) -> q s", q=DS),
                         allow_slow_non_contiguous=True).then_inc(S("wcol_in"), 16)
        sp.wait_ge(S("turned1"), upto("turned1", 25))
        sp.wait_ge(S("wi_out"), 16)
        for s in range(NS):
            if s >= 2:
                sp.wait_ge(S("idx_s_mm"), s - 1)
            for j in range(NPG):
                sp.dma_start(g3(at("CR", 1024 * (s % 2), 1024, 0, 64), NPG)[:, j, :],
                             page_rows(a["kidx_t"], page_id(s, j)))\
                    .then_inc(S(f"kidx{s % 2}"), 16)
        for s in range(NS):
            if s == 0:
                sp.wait_ge(S("idx_s_mm"), NS)
                sp.wait_ge(S("odd_out"), 16 * 6)
            if s == 2:
                sp.wait_ge(S("sel"), 1)
            if s >= 3:
                sp.wait_ge(S("pv_s1"), upto("pv_s1", s - 2))
            for j in range(NPG):
                sp.dma_start(g3(kv_odd[s % 3], NPG)[:, j, :], page_rows(a["dsa_page"], page_id(s, j)))\
                    .then_inc(S(f"kv{s % 3}"), 16)
            if s >= 2:
                sp.wait_ge(S("pv_s1"), upto("pv_s1", s - 1))
            if s == 0:
                sp.wait_ge(S("pv1"), upto("pv1", HC))
            sp.dma_start(vnew[1][s % 2],
                         o["dsa_v_sample"][0, s].rearrange("j g d -> j (g d)"))\
                .then_inc(S(f"vnew1_{s % 2}"), 16)
        sp.wait_ge(S("pv_s1"), upto("pv_s1", NS))
        stream(first_block(1, "moe"))
        experts(1)
        spilled(1)
        sp.wait_ge(S("combined1"), upto("combined1", 1))
        sp.dma_start(fin_g, a["fin_gain"]).then_inc(S("c_fin"), 16)
        for t, c0, c1 in TILES:
            sp.wait_ge(S("y_ready"), t + 1)
            dst = o["y_prompt"][0, c0:c1, :] if t < 4 else o["y_sample"].rearrange("s j d -> (s j) d")
            sp.dma_start(dst, yfin[t % 2][0:rows(t), :]).then_inc(S(f"y_out{t % 2}"), 16)
        sp.wait_ge(S("y_out0"), 48)
        sp.wait_ge(S("y_out1"), 32)

    @block.gpsimd
    def _(pool):
        for i in (0, 2):
            pool.memset(tick[i], 0.0).then_inc(S("pads"), 1)
        pool.memset(zeros, 0.0).then_inc(S("zeros"), 1)
        pool.wait_ge(S("zeros"), 1)
        pool.dma_start(y_d[NE * CAP:, :].rearrange("(s p) d -> p s d", p=128),
                       bc_mid(zeros, SPILLS))\
            .then_inc(S("zeros_out"), 16)
        pool.memset(ucp[:, :, 0:30], 0.0).then_inc(S("pads"), 1)
        pool.memset(lft[:, :, :], 0.0).then_inc(S("pads"), 1)

        def both(names, buf, c0, c1, axes, sem):
            pool.dma_start(o[names + "_prompt"].rearrange(axes[0], p=128), buf[:, 0:4, c0:c1]).then_inc(S(sem), 16)
            pool.dma_start(o[names + "_sample"].rearrange(axes[1]), buf[0:NSAMP, 4, c0:c1]).then_inc(S(sem), 16)

        AX = ("a b (t p) h d -> p (a b t) (h d)", "a s j h d -> (a s j) (h d)")
        pool.wait_ge(S("u_ready"), 5)
        pool.dma_start(o["conv_state_prompt"][0, 0], A0[98:128, 3, 0:512]).then_inc(S("u_out"), 16)
        for s in range(NS):
            pool.dma_start(o["conv_state_sample"][0, s, 22:30, :],
                           A0[8 * s:8 * s + 8, 4, 0:512])\
                .then_inc(S("u_out"), 16)
        pool.dma_start(o["conv_state_sample"][0, :, 0:22, :], a["state_conv"][:, 8:30, :]).then_inc(S("state_out"), 16)
        pool.wait_ge(S("c_small"), 16)
        pool.wait_ge(S("turn_ev0"), 5)
        u4 = ucs[:, :, :].rearrange("p c (s w) -> p c s w", s=NS)
        out4 = conv_s.rearrange("p c (s w) -> p c s w", s=NS)
        for j in range(CW):
            product = tap[j % 2].rearrange("p (c s w) -> p c s w", c=4, s=NS)
            w = wdw[:, :, j:j + 1].unsqueeze(3).broadcast_to([128, 4, NS, DS])
            before = bdw.unsqueeze(2).unsqueeze(3).broadcast_to([128, 4, NS, DS]) if j == 0 else out4
            pool.tensor_tensor(product, u4[:, :, :, j:j + DS], w, ALU.mult).then_inc(S("conv_tap"), 1)
            pool.wait_ge(S("conv_tap"), 2 * j + 1)
            pool.tensor_tensor(out4, before, product, ALU.add).then_inc(S("conv_tap"), 1)
        pool.wait_ge(S("proj_ev0"), 20)
        both("fox_k", A2, 0, 512, AX, "fox_k_out")
        pool.wait_ge(S("proj_ev0"), 25)
        both("fox_v", A3, 0, 512, AX, "fox_v_out")
        pool.wait_ge(S("logf"), 1)
        pool.dma_start(o["fox_logf_prompt"].rearrange("a b (t p) h -> p (a b t) h", p=128),
                       lft[:, 0:4, :])\
            .then_inc(S("logf_out"), 16)
        pool.dma_start(o["fox_logf_sample"].rearrange("a s j h -> (a s j) h"),
                       lft[0:NSAMP, 4, :])\
            .then_inc(S("logf_out"), 16)

        def norm_rows(l):
            for t, c0, c1 in TILES:
                pool.wait_ge(S(f"hn{2 * l + 1}"), upto(f"hn{2 * l + 1}", t + 1))
                pool.dma_start(hn_d[c0:c1, :], hn[t % 2][0:rows(t), :]).then_inc(S(f"hn_out{l}_{t % 2}"), 16)

        def after_wait(cell):
            return pool.tensor_tensor(cell, cell, cell, ALU.mult)

        def gather(l, n, par):
            if past(n - 1):
                pool.wait_ge(S(f"xg_used{l}"), upto(f"xg_used{l}", n - 1))
            pool.tensor_copy(idxc[par], tok_u[:, bass.ds(n, 1)] if not isinstance(n, int) else tok_u[:, n:n + 1])\
                .then_inc(S(f"idx{l}"), 1)
            pool.wait_ge(S(f"idx{l}"), upto(f"idx{l}", n + 1))
            after_wait(tick[0])
            pool.indirect_dma_start(xg[par], None, hn_d, bass.IndirectOffsetOnAxis(idxc[par], 0))\
                .then_inc(S(f"xg{l}_{par}"), 16)

        def experts(l):
            pool.wait_ge(S(f"tok{l}"), upto(f"tok{l}", 1))
            pool.wait_ge(S(f"hn_out{l}_0"), upto(f"hn_out{l}_0", 48))
            pool.wait_ge(S(f"hn_out{l}_1"), upto(f"hn_out{l}_1", 32))
            for n in range(4):
                gather(l, n, n % 2)
            with pool.Fori(2, NE // 2) as i:
                for par in range(2):
                    gather(l, 2 * i + par, par)

        def spilled(l):
            pool.wait_ge(S(f"turns{l}"), upto(f"turns{l}", 1))

            def turn(n):
                pool.wait_ge(S(f"general{l}_"), n * TURN + STEPS["token"])
                after_wait(tick[2]).then_inc(S(f"general{l}_"), 1)
                pool.indirect_dma_start(xg[0], None, hn_d, bass.IndirectOffsetOnAxis(idxc[0], 0))\
                    .then_inc(S(f"general_x{l}_"), 16)
                pool.wait_ge(S(f"general{l}_"), n * TURN + STEPS["stored"])
                after_wait(tick[2]).then_inc(S(f"general{l}_"), 1)

            further_rounds(pool, turn)

        def combine(l):
            pool.wait_ge(S(f"row_u{l}"), upto(f"row_u{l}", 1))
            pool.wait_ge(S(f"y_rows{l}_0"), upto(f"y_rows{l}_0", 16 * NE // 2))
            pool.wait_ge(S(f"y_rows{l}_1"), upto(f"y_rows{l}_1", 16 * NE // 2))
            for t in range(NT):
                if t - 1 > 0:
                    pool.wait_ge(S(f"combined{l}"), upto(f"combined{l}", t - 1))
                for k in range(2):
                    i = (2 * t + k) % 4
                    pool.indirect_dma_start(ybuf[i][0:rows(t), :], None, y_d,
                                            bass.IndirectOffsetOnAxis(row_u[0:rows(t), NT * k + t:NT * k + t + 1], 0))\
                        .then_inc(S(f"yb{l}_{i}"), 16)

        norm_rows(0)
        experts(0)
        spilled(0)
        combine(0)
        pool.wait_ge(S("roped"), 5 * NT)
        both("dsa_k", A3, 0, 256, AX, "odd_out")
        both("dsa_v", A3, 256, 512, AX, "odd_out")
        pool.dma_start(o["dsa_kidx_prompt"].rearrange("a b (t p) d -> p (a b t) d", p=128),
                       tail_odd[:, 0:4, 0:64])\
            .then_inc(S("odd_out"), 16)
        pool.dma_start(o["dsa_kidx_sample"].rearrange("a s j d -> (a s j) d"),
                       tail_odd[0:NSAMP, 4, 0:64])\
            .then_inc(S("odd_out"), 16)
        pool.dma_start(wi_d, tail_odd[0:NSAMP, 4, 64:72]).then_inc(S("wi_out"), 16)
        norm_rows(1)
        experts(1)
        spilled(1)
        combine(1)
        for name, n in (("state_out", 1), ("fox_k_out", 2)):
            pool.wait_ge(S(name), upto(name, 16 * n))

    @block.tensor
    def _(pe):
        mm = pe.matmul

        def norm(n):
            if n == 0:
                pe.wait_ge(S("c_ident"), 16)
            for t, c0, c1 in TILES:
                pe.wait_ge(S(f"hn{n}"), upto(f"hn{n}", t + 1))
                if t - 1 > 0:
                    pe.wait_ge(S(f"xt{n}"), upto(f"xt{n}", t - 1))
                for c in range(DC):
                    b = 4 + 2 * (t % 2) + c // 4
                    last = pe.transpose(bank(b, 128 * (c % 4), 128 * (c % 4) + rows(t)),
                                        hn[t % 2][0:rows(t), 128 * c:128 * c + 128], ident[0:rows(t), 0:rows(t)])
                last.then_inc(S(f"hn_t{n}"), 1)
                if n % 2 and t:
                    route_tile(n // 2, t - 1)
            if n % 2:
                route_tile(n // 2, NT - 1)

        def route_tile(l, t):
            if t == 0:
                pe.wait_ge(S("c_misc"), 16 * 6)
                pe.wait_ge(S(f"out_add{l}"), upto(f"out_add{l}", 7))
            pe.wait_ge(S(f"xt{2 * l + 1}"), upto(f"xt{2 * l + 1}", t + 1))
            for c in range(DC):
                last = mm(bank(2, 20 * t, 20 * t + 20, 0, rows(t)), xt[:, c, 128 * t:128 * t + rows(t)],
                          wrout[l][:, c, :], start=(c == 0), stop=(c == DC - 1))
            if t == NT - 1:
                last.then_inc(S(f"route_mm{l}"), 1)

        def project(l, after=None):
            for b in range(NBLK[l]):
                k = first_block(l, "in") + b
                pe.wait_ge(S(f"ring{k % RING}"), 16 * (k // RING + 1))
                w = g3(ring[k % RING], DC)
                for t, c0, c1 in TILES:
                    if b == 0:
                        pe.wait_ge(S(f"xt{2 * l}"), upto(f"xt{2 * l}", t + 1))
                    job = 5 * b + t
                    if job - 3 > 0:
                        pe.wait_ge(S(f"proj_ev{l}"), upto(f"proj_ev{l}", job - 3))
                    for c in range(DC):
                        last = mm(bank(job % 4, 0, 512, 0, rows(t)), xt[:, c, c0:c1], w[:, c, :],
                                  start=(c == 0), stop=(c == DC - 1))
                    last.then_inc(S(f"proj_mm{l}"), 1)
                    if after:
                        after(job)
            pe.wait_ge(S(f"c_tail{l}"), 16)
            for t, c0, c1 in TILES:
                for c in range(DC):
                    last = mm(bank(4, TAIL[l] * t, TAIL[l] * (t + 1), 0, rows(t)), xt[:, c, c0:c1], wtail[l][:, c, :],
                              start=(c == 0), stop=(c == DC - 1))
            last.then_inc(S(f"tail_mm{l}"), 1)

        def turn(l, job, src):
            if job - 2 > 0:
                pe.wait_ge(S(f"turn_ev{l}"), upto(f"turn_ev{l}", job - 2))
            for i, piece in enumerate(src):
                r = piece.shape[0]
                last = pe.transpose(bank(5 + job % 3, 128 * i, 128 * i + r), piece, ident[0:r, 0:r])
            last.then_inc(S(f"turned{l}"), 1)

        def scores_p(l, j, heads, q, k):
            t, hh = j % 4, j // 4
            if j - 2 > 0:
                pe.wait_ge(S(f"sb{l}"), upto(f"sb{l}", j - 2))
            n = 128 * (t + 1)
            qa, ka = q(hh), k(hh)
            last = mm(bank(S_BANK[j % 3], 0, n), qa[:, 128 * t:128 * t + 128], ka[:, 0:n], start=True, stop=(l == 1))
            if l == 0:
                last = mm(bank(S_BANK[j % 3], 0, n), ident[0:8, hh:hh + 1].broadcast_to([8, 128]), ckp[0:8, 0:n],
                          start=False, stop=True)
            last.then_inc(S(f"s_mm{l}"), 1)

        def turn_p(l, j):
            t = j % 4
            pe.wait_ge(S(f"probs{l}"), upto(f"probs{l}", j + 1))
            if j - 1 > 0:
                pe.wait_ge(S(f"pt_ev{l}"), upto(f"pt_ev{l}", j - 1))
            for kt in range(t + 1):
                last = pe.transpose(bank(2 + j % 2, 128 * kt, 128 * kt + 128), sb[l][j % 3][:, 128 * kt:128 * kt + 128],
                                    ident)
            last.then_inc(S(f"p_turned{l}"), 1)

        def values_p(l, hh, v):
            pe.wait_ge(S(f"pt_ev{l}"), upto(f"pt_ev{l}", 4 * (hh + 1)))
            if hh - 1 > 0:
                pe.wait_ge(S(f"o_ev{l}"), upto(f"o_ev{l}", hh - 1))
            p0 = 64 * (hh % 2)
            for kt in range(4):
                last = mm(bank(4 + hh % 2, 128 * kt, 512, p0, p0 + 64), v(hh, kt), pt[hh % 2][:, kt, 128 * kt:512],
                          start=(kt == 0), stop=(kt == 3))
            last.then_inc(S(f"pv{l}"), 1)

        def attend_p(l, heads, q, k, v):
            scores_p(l, 0, heads, q, k)
            scores_p(l, 1, heads, q, k)
            for j in range(4 * heads):
                if j + 2 < 4 * heads:
                    scores_p(l, j + 2, heads, q, k)
                turn_p(l, j)
                if j % 4 == 2 and j > 4:
                    values_p(l, j // 4 - 1, v)
            values_p(l, heads - 1, v)

        def attend_s(l, R, nc_, qb, keys, new_k, bias_l, bias_r, vals, W):
            def score(s):
                if l == 0:
                    pe.wait_ge(S(f"kv{s % 2}"), 128 * (s // 2 + 1))
                else:
                    pe.wait_ge(S(f"kv{s % 3}"), 64 * NS + 128 * (s // 3 + 1))
                if s > 0:
                    pe.wait_ge(S(f"exp_s{l}"), upto(f"exp_s{l}", s))
                for b in range(2):
                    for c in range(nc_):
                        mm(bank(b, 0, 512, 0, R), qb[:, c, s, :], keys(s, b, c), start=(c == 0), stop=False)
                    mm(bank(b, 0, 512, 0, R), bias_l(s), bias_r[:, 512 * b:512 * b + 512], start=False, stop=True)
                for c in range(nc_):
                    mm(bank(2, 0, 8, 0, R), qb[:, c, s, :], new_k(s, c), start=(c == 0), stop=False)
                mm(bank(2, 0, 8, 0, R), bias_l(s), bias_r[:, 1024:LK], start=False, stop=True)\
                    .then_inc(S(f"scored{l}"), 1)

            def turn_s(s):
                pe.wait_ge(S(f"exp_s{l}"), upto(f"exp_s{l}", s + 1))
                for g in range(3):
                    if 3 * (s - 1) + g + 1 > 0:
                        pe.wait_ge(S(f"pts_ev{l}"), upto(f"pts_ev{l}", 3 * (s - 1) + g + 1))
                    for i in range(4 if g < 2 else 1):
                        kt = 4 * g + i
                        w = 128 if kt < 8 else 8
                        last = pe.transpose(bank((3, 4, 7)[g], R * i, R * i + R, 0, w),
                                            prs[s % 2][0:R, 128 * kt:128 * kt + w], ident[0:R, 0:R])
                    last.then_inc(S(f"ps_turned{l}"), 1)

            def value(s):
                pe.wait_ge(S(f"pts_ev{l}"), upto(f"pts_ev{l}", 3 * (s + 1)))
                if s > 0:
                    pe.wait_ge(S(f"osum{l}"), upto(f"osum{l}", s))
                if l == 0:
                    pe.wait_ge(S(f"kv{2 + s % 2}"), 128 * (s // 2 + 1))
                pe.wait_ge(S(f"vnew{l}_{s % 2}"), upto(f"vnew{l}_{s % 2}", 16 * (s // 2 + 1)))
                for kt in range(8):
                    mm(bank(5, 0, W, 0, R), pts[s % 2][:, R * kt:R * kt + R], vals(s, kt), start=(kt == 0), stop=False)
                mm(bank(5, 0, W, 0, R), pts[s % 2][0:8, 8 * R:9 * R], vnew[l][s % 2], start=False, stop=True)\
                    .then_inc(S(f"pv_s{l}"), 1)

            def turn_o(s):
                pe.wait_ge(S(f"osum{l}"), upto(f"osum{l}", s + 1))
                if s > 0:
                    pe.wait_ge(S(f"os_ev{l}"), upto(f"os_ev{l}", s))
                pe.transpose(bank(6, 0, R), o2[0:R, :], ident[0:R, 0:R]).then_inc(S(f"o_turned{l}"), 1)

            score(0)
            for s in range(NS):
                turn_s(s)
                if s + 1 < NS:
                    score(s + 1)
                value(s)
                if s:
                    turn_o(s - 1)
            turn_o(NS - 1)

        def out_project(l):
            pe.wait_ge(S(f"os_ev{l}"), upto(f"os_ev{l}", NS))
            pe.wait_ge(S(f"o_ev{l}"), upto(f"o_ev{l}", (HB, HC)[l]))
            if l == 0:
                pe.wait_ge(S("a_out"), 4)
            for b in range(2):
                k = first_block(l, "out") + b
                pe.wait_ge(S(f"ring{k % RING}"), 16 * (k // RING + 1))
                w = g3(ring[k % RING], DC)
                for t, c0, c1 in TILES:
                    job = 5 * b + t
                    if job - 3 > 0:
                        pe.wait_ge(S(f"out_add{l}"), upto(f"out_add{l}", job - 3))
                    for c in range(DC):
                        last = mm(bank(job % 4, 0, 512, 0, rows(t)), xt[:, c, c0:c1], w[:, c, :],
                                  start=(c == 0), stop=(c == DC - 1))
                    last.then_inc(S(f"out_mm{l}"), 1)

        def route(l):
            pe.wait_ge(S(f"out_add{l}"), upto(f"out_add{l}", 10))
            pe.wait_ge(S(f"mask{l}"), upto(f"mask{l}", 1))
            for t in range(NT):
                for s in range(t + 1):
                    mm(bank(1, NE * t, NE * t + NE), before16 if s == t else ones16, mask16[:, s, :],
                       start=(s == 0), stop=(s == t))
            for s in range(NT):
                last = mm(bank(2, 0, NE), ones16, mask16[:, s, :], start=(s == 0), stop=(s == NT - 1))
            last.then_inc(S(f"pos_mm{l}"), 1)
            for t in range(NT):
                pe.wait_ge(S(f"dmat{l}"), upto(f"dmat{l}", t + 1))
                for e in range(NE):
                    last = mm(bank(3, e, e + 1), dmat[t % 2][:, e, :], tokid16[:, t:t + 1],
                              start=(t == 0 and e == 0), stop=(t == NT - 1), skip_group_check=True)
                last.then_inc(S(f"tok_mm{l}"), 1)

        def turn_x(l, n, par):
            pe.wait_ge(S(f"xg{l}_{par}"), upto(f"xg{l}_{par}", n * 8 + (16 - 8 * par)))
            if past(n):
                pe.wait_ge(S(f"xgt{l}"), upto(f"xgt{l}", n))
            for c in range(DC):
                last = pe.transpose(bank(6 + c // 4, 128 * (c % 4), 128 * (c % 4) + 128),
                                    xg[par][:, 128 * c:128 * c + 128], ident)
            last.then_inc(S(f"xg_used{l}"), 1)

        def expert(l, n, par, last_one=False):
            b = first_block(l, "moe")

            def here(i):
                return ring[(b + i) % RING]

            def landed(i):
                pe.wait_ge(S(f"ring{(b + i) % RING}"), n * 16 + 16 * ((b + i) // RING + 1))

            pe.wait_ge(S(f"xgt{l}"), upto(f"xgt{l}", n + 1))
            landed(0)
            if past(n):
                pe.wait_ge(S(f"silu{l}"), upto(f"silu{l}", n))
            for c in range(DC):
                last = mm(bank(0), xgt[par][:, c, :], g3(here(0), DC)[:, c, :], start=(c == 0), stop=(c == DC - 1))
            last.then_inc(S(f"gate_mm{l}"), 1)
            landed(1)
            if past(n):
                pe.wait_ge(S(f"hid{l}"), upto(f"hid{l}", n))
            for c in range(DC):
                last = mm(bank(1), xgt[par][:, c, :], g3(here(1), DC)[:, c, :], start=(c == 0), stop=(c == DC - 1))
            last.then_inc(S(f"up_mm{l}"), 1)
            if not last_one:
                turn_x(l, n + 1, 1 - par)
            pe.wait_ge(S(f"hid{l}"), upto(f"hid{l}", n + 1))
            if past(n):
                pe.wait_ge(S(f"hidt{l}"), upto(f"hidt{l}", n))
            for c in range(4):
                last = pe.transpose(bank(2, 128 * c, 128 * c + 128), hid[:, 128 * c:128 * c + 128], ident)
            last.then_inc(S(f"hid_turned{l}"), 1)
            pe.wait_ge(S(f"hidt{l}"), upto(f"hidt{l}", n + 1))
            landed(2)
            if past(n):
                pe.wait_ge(S(f"y_a{l}"), upto(f"y_a{l}", n))
            if past(n):
                pe.wait_ge(S(f"y_v{l}"), upto(f"y_v{l}", n))
            for c2 in range(2):
                for c in range(4):
                    last = mm(bank(3 + c2), hidt[:, c, :], g3(here(2), 4)[:, c, 512 * c2:512 * c2 + 512],
                              start=(c == 0), stop=(c == 3))
            last.then_inc(S(f"down_mm{l}"), 1)

        def experts(l):
            pe.wait_ge(S(f"tok{l}"), upto(f"tok{l}", 1))
            turn_x(l, 0, 0)
            for n in range(2):
                expert(l, n, n % 2)
            with pe.Fori(1, NE // 2 - 1) as i:
                for par in range(2):
                    expert(l, 2 * i + par, par)
            for n in range(NE - 2, NE):
                expert(l, n, n % 2, n == NE - 1)

        def spilled(l):
            pe.wait_ge(S(f"turns{l}"), upto(f"turns{l}", 1))
            pe.wait_ge(S(f"y_a{l}"), upto(f"y_a{l}", NE))
            pe.wait_ge(S(f"y_v{l}"), upto(f"y_v{l}", NE))

            def turn(n):
                pe.wait_ge(S(f"general{l}_"), n * TURN + STEPS["places"])
                for k in range(2):
                    for t in range(NT):
                        last = mm(bank(3, 0, 1), places[k][:, t, :], tokid16[:, t:t + 1],
                                  start=(k == 0 and t == 0), stop=(k == 1 and t == NT - 1))
                last.then_inc(S(f"general{l}_"), 1)
                pe.wait_ge(S(f"general_x{l}_"), 16 * n + 16)
                for c in range(DC):
                    last = pe.transpose(bank(6 + c // 4, 128 * (c % 4), 128 * (c % 4) + 128),
                                        xg[0][:, 128 * c:128 * c + 128], ident)
                last.then_inc(S(f"general{l}_"), 1)
                pe.wait_ge(S(f"general{l}_"), n * TURN + STEPS["inputs"])
                pe.wait_ge(S(f"general_w{l}_"), 48 * n + 48)
                for i in range(2):
                    for c in range(DC):
                        last = mm(bank(i), xgt[0][:, c, :], g3(over_w[i], DC)[:, c, :],
                                  start=(c == 0), stop=(c == DC - 1))
                last.then_inc(S(f"general{l}_"), 1)
                pe.wait_ge(S(f"general{l}_"), n * TURN + STEPS["hid"])
                for c in range(4):
                    last = pe.transpose(bank(2, 128 * c, 128 * c + 128), hid[:, 128 * c:128 * c + 128], ident)
                last.then_inc(S(f"general{l}_"), 1)
                pe.wait_ge(S(f"general{l}_"), n * TURN + STEPS["hidt"])
                for c2 in range(2):
                    for c in range(4):
                        last = mm(bank(4 + c2), hidt[:, c, :], g3(over_w[2], 4)[:, c, 512 * c2:512 * c2 + 512],
                                  start=(c == 0), stop=(c == 3))
                last.then_inc(S(f"general{l}_"), 1)

            further_rounds(pe, turn)

        norm(0)

        def turn_u(job):
            for t in U_TURNS.get(job, ()):
                pe.wait_ge(S("u_ready"), t + 1)
                turn(0, t, [A0[0:rows(t), t, 128 * i:128 * i + 128] for i in range(4)])

        project(0, turn_u)
        for job in range(5, 15):
            kind, t = job // 5, job % 5
            if t == 0:
                pe.wait_ge(S("proj_ev0"), 5 * kind + 10)
            src = (None, A1, A2)[kind]
            turn(0, job, [src[0:rows(t), t, 128 * i:128 * i + 128] for i in range(4)])
        pe.wait_ge(S("logf"), 1)
        pe.wait_ge(S("c_even"), 16 * 4)
        for i in range(4):
            last = mm(bank(4, 128 * i, 512, 0, 8), lft[:, i, :], tri[:, 0:512 - 128 * i], start=(i == 0), stop=(i == 3))
        last.then_inc(S("cum_mm"), 1)
        pe.wait_ge(S("lf_in"), 16 * NS * NPG)
        pe.wait_ge(S("nlf_in"), 16)
        for i in range(NPG):
            for b in range(3):
                lo, hi = max(512 * b, 128 * i), min(512 * b + 512, LK)
                if lo < hi:
                    mm(bank(b, lo - 512 * b, hi - 512 * b, 0, 64), lfa[:, i, :], tri[:, lo - 128 * i:hi - 128 * i],
                       start=(i == 0), stop=(b < 2 and 128 * (i + 1) == min(512 * (b + 1), PAST)))
        mm(bank(2, 0, 8, 0, 64), nlf, tri[0:8, 0:8], start=False, stop=True).then_inc(S("cum_mm"), 1)
        pe.wait_ge(S("cum_ev"), 2)
        pe.wait_ge(S("conv"), 1)
        pe.wait_ge(S("conv_tap"), 2 * CW)
        for (b0, b1, src, name) in ((0, 1, lambda c, x0, x1: (conv_s if x0 else conv_p)[:, c, :], "ln_mm"),
                                    (2, 3, lambda c, x0, x1: sqv[:, c, x0:x1], "ln_mm")):
            if b0:
                pe.wait_ge(S("squares"), 1)
            for c in range(4):
                mm(bank(b0), mean_m, src(c, 0, 512), start=(c == 0), stop=(c == 3))
            for c in range(4):
                last = mm(bank(b1, 0, 64), mean_m, src(c, 512, TOK), start=(c == 0), stop=(c == 3))
            last.then_inc(S(name), 1)
        pe.wait_ge(S("ln_var"), 1)
        pe.wait_ge(S("cum_ev"), 1)

        def rows64(base, chunk, par):
            return base[64 * par:64 * par + 64, chunk, :]

        attend_p(0, HB, lambda hh: rows64(qt, hh // 2, hh % 2), lambda hh: rows64(qt, 4 + hh // 2, hh % 2),
                 lambda hh, kt: A3[:, kt, 64 * hh:64 * hh + 64])
        pe.wait_ge(S("qbd0"), 1)
        pe.wait_ge(S("o_ev0"), HB)
        pe.wait_ge(S("pt_ev0"), 4 * HB)
        attend_s(0, 64, 4, qbd_even,
                 lambda s, b, c: g3(k_even[s % 2], NPG)[:, 4 * b:4 * b + 4, 128 * c:128 * c + 128],
                 lambda s, c: qt[:, 4 + c, SEQ + 8 * s:SEQ + 8 * s + 8],
                 lambda s: self_[:, s, :], cks[0:72, :],
                 lambda s, kt: g3(v_even[s % 2], NPG)[:, kt, :], 512)
        out_project(0)
        norm(1)
        route(0)
        experts(0)
        spilled(0)
        norm(2)
        project(1)
        job = 0
        for t in range(NT):
            pe.wait_ge(S("roped"), 3 * NT + 2 * t + 2)
            r = rows(t)
            a0, a3, a1 = A0[0:r, t, :], A3[0:r, t, :], A1[0:r, t, :]
            for src in ([a0[:, 128 * i:128 * i + 128] for i in range(4)],
                        [a0[:, 128 * i:128 * i + 128] for i in range(4, 8)],
                        [kdup[t % 2][0:r, 128 * g:128 * g + 128] for g in range(4)],
                        [a1[:, 128 * i:128 * i + 128] for i in range(4)],
                        [kdup[t % 2][0:r, 512:640]]):
                turn(1, job, src)
                job += 1
        job = 0
        pe.wait_ge(S("turn_ev1"), upto("turn_ev1", 25))
        for t in range(1, 4):
            for hh in range(HI):
                if job - 3 > 0:
                    pe.wait_ge(S("relu"), job - 3)
                mm(bank(job % 4, 0, 128 * (t + 1)), rows64(qi, hh // 2, hh % 2)[:, 128 * t:128 * t + 128],
                   ki[64 * (hh % 2):64 * (hh % 2) + 64, 0:128 * (t + 1)], start=True, stop=True)\
                    .then_inc(S("idx_mm"), 1)
                job += 1
        pe.wait_ge(S("relu"), 24)
        pe.wait_ge(S("qis"), 1)
        pe.wait_ge(S("c_odd"), 48)
        for s in range(NS):
            pe.wait_ge(S(f"kidx{s % 2}"), 128 * (s // 2 + 1))
            if s > 0:
                pe.wait_ge(S("relu_s"), s)
            for b in range(2):
                mm(bank(b, 0, 512, 0, 64), qis[:, 64 * s:64 * s + 64],
                   at("CR", 1024 * (s % 2) + 512 * b, 512, 0, 64), start=True, stop=True)
            mm(bank(2, 0, 8, 0, 64), qis[:, 64 * s:64 * s + 64], ki[0:64, SEQ + 8 * s:SEQ + 8 * s + 8],
               start=True, stop=True).then_inc(S("idx_s_mm"), 1)
            pe.wait_ge(S("relu_s"), s + 1)
            for b, (x0, x1) in enumerate(((0, 512), (512, 1024), (1024, LK))):
                last = mm(bank(4 + b, 0, x1 - x0, 0, 64), ohw[:, 56 - 8 * s:120 - 8 * s], rw[:, x0:x1],
                          start=(s == 0), stop=(s == NS - 1))
            last.then_inc(S("idx_sum"), 1)
        pe.wait_ge(S("qbd1"), upto("qbd1", 1))
        attend_p(1, HC, lambda hh: rows64(qt, hh // 2, hh % 2), lambda hh: rows64(kd, hh // 4, hh % 2),
                 lambda hh, kt: A3[:, kt, 256 + 64 * (hh // 4):320 + 64 * (hh // 4)])
        pe.wait_ge(S("o_ev1"), upto("o_ev1", HC))
        pe.wait_ge(S("pt_ev1"), upto("pt_ev1", 4 * HC))
        pe.wait_ge(S("sel"), 1)
        attend_s(1, 128, 2, qbd_odd,
                 lambda s, b, c: g3(kv_odd[s % 3], NPG)[:, 4 * b:4 * b + 4, 128 * c:128 * c + 128],
                 lambda s, c: k_new_odd[:, c, 8 * s:8 * s + 8],
                 lambda s: es[:, s, :], sels,
                 lambda s, kt: g3(kv_odd[s % 3], NPG)[:, kt, 256:512], 256)
        out_project(1)
        norm(3)
        route(1)
        experts(1)
        spilled(1)

    @block.scalar
    def _(act):
        af = act.activation

        def norm(n):
            act.wait_ge(S("init"), 1)
            for t, c0, c1 in TILES:
                h_ready(act, n, t)
                if t > 0:
                    act.wait_ge(S(f"sq{n}"), upto(f"sq{n}", t))
                af(junk[0:rows(t), :], h[0:rows(t), t, :], ACT.Square, accum_out=ssq[0:rows(t), t:t + 1])\
                    .then_inc(S(f"sq{n}"), 1)
            act.wait_ge(S(f"ms{n}"), upto(f"ms{n}", 1))
            af(rstd, rstd, ACT.Sqrt).then_inc(S(f"root{n}"), 1)

        def turned(job):
            kind, t = job // 5, job % 5
            if job == 0:
                act.wait_ge(S("pads"), 4)
                act.wait_ge(S("c_even"), 64)
            act.wait_ge(S("turned0"), job + 1)
            src = g3(bank(5 + job % 3), 4)[:, :, 0:rows(t)]
            if kind == 0 and t < 4:
                dst = ucp[:, :, 30 + 128 * t:158 + 128 * t]
            elif kind == 0:
                dst = ucs[:, :, :].rearrange("p c (s w) -> p c s w", s=NS)[:, :, :, 30:38]
                src = src.rearrange("p c (s i) -> p c s i", s=NS)
            else:
                dst = qt[:, 4 * kind - 4:4 * kind, 128 * t:128 * t + rows(t)]
            af(dst, src, ACT.Copy).then_inc(S("turn_ev0"), 1)

        def project(l):
            for job in range(5 * NBLK[l]):
                b, t = job // 5, job % 5
                if l == 0:
                    dst, f, sc = ((A0[:, t, 0:512], ACT.Copy, 1.0), (A0[:, t, 512:1024], ACT.Sigmoid, 1.0),
                                  (A1[:, t, :], ACT.Copy, 0.125), (A2[:, t, :], ACT.Copy, 1.0),
                                  (A3[:, t, :], ACT.Copy, 1.0))[b]
                else:
                    dst, f, sc = ((A0[:, t, 0:512], ACT.Copy, 0.125), (A0[:, t, 512:1024], ACT.Copy, 0.125),
                                  (A3[:, t, :], ACT.Copy, 1.0), (A1[:, t, :], ACT.Copy, 0.125))[b]
                act.wait_ge(S(f"proj_mm{l}"), upto(f"proj_mm{l}", job + 1))
                if l == 0 and job == 20:
                    act.wait_ge(S("zeros_out"), 16)
                af(dst[0:rows(t)], bank(job % 4, 0, 512, 0, rows(t)), f, scale=sc).then_inc(S(f"proj_ev{l}"), 1)
                if l == 0:
                    for t in U_TURNS.get(job, ()):
                        turned(t)
            act.wait_ge(S(f"tail_mm{l}"), upto(f"tail_mm{l}", 1))
            w = TAIL[l]
            dst = lft if l == 0 else tail_odd
            af(dst[:, 0:4, :], g3(bank(4, 0, 4 * w), 4), ACT.Copy).then_inc(S(f"tail_ev{l}"), 1)
            af(dst[0:NSAMP, 4, :], bank(4, 4 * w, 5 * w, 0, NSAMP), ACT.Copy).then_inc(S(f"tail_ev{l}"), 1)

        def prompt(l, heads, chunk0):
            def evac(j):
                t, hh = j % 4, j // 4
                act.wait_ge(S(f"p_turned{l}"), upto(f"p_turned{l}", j + 1))
                if t == 0:
                    if hh - 1 > 0:
                        act.wait_ge(S(f"pv{l}"), upto(f"pv{l}", hh - 1))
                n = 128 * (t + 1)
                af(pt[hh % 2][:, 0:t + 1, 128 * t:128 * t + 128], g3(bank(2 + j % 2, 0, n), t + 1), ACT.Copy)\
                    .then_inc(S(f"pt_ev{l}"), 1)

            for j in range(4 * heads):
                n = 128 * (j % 4 + 1)
                act.wait_ge(S(f"nmx{l}"), upto(f"nmx{l}", j + 1))
                af(sb[l][j % 3][:, 0:n], sb[l][j % 3][:, 0:n], ACT.Exp, bias=nmx[:, j % 3:j % 3 + 1],
                   accum_out=esum[:, j % 3:j % 3 + 1]).then_inc(S(f"exp{l}"), 1)
                if j >= 2:
                    evac(j - 2)
            evac(4 * heads - 2)
            evac(4 * heads - 1)

        def samples(l, R, chunk0, nch):
            def exps(s):
                act.wait_ge(S(f"nmx_s{l}"), upto(f"nmx_s{l}", s + 1))
                if 3 * (s - 1) > 0:
                    act.wait_ge(S(f"ps_turned{l}"), upto(f"ps_turned{l}", 3 * (s - 1)))
                af(prs[s % 2][0:R, :], psum[0:R, 0:LK], ACT.Exp, bias=nmx[0:R, s % 2:s % 2 + 1],
                   accum_out=esum[0:R, s % 2:s % 2 + 1]).then_inc(S(f"exp_s{l}"), 1)

            def evac_o(s):
                act.wait_ge(S(f"o_turned{l}"), upto(f"o_turned{l}", s + 1))
                for par in range(2):
                    src = bank(6, 0, R, 64 * par, 64 * par + 64).rearrange("p (c a q) -> p c a q", a=2, q=DS)
                    last = af(xt[64 * par:64 * par + 64, chunk0:chunk0 + nch, SEQ + 8 * s:SEQ + 8 * s + 8],
                              src[:, :, par, :], ACT.Copy)
                last.then_inc(S(f"os_ev{l}"), 1)

            exps(0)
            for s in range(NS):
                for g in range(3):
                    act.wait_ge(S(f"ps_turned{l}"), upto(f"ps_turned{l}", 3 * s + g + 1))
                    if g == 0:
                        if s - 1 > 0:
                            act.wait_ge(S(f"pv_s{l}"), upto(f"pv_s{l}", s - 1))
                    r = 128 if g < 2 else 8
                    n = 4 * R if g < 2 else R
                    af(pts[s % 2][0:r, 4 * R * g:4 * R * g + n], bank((3, 4, 7)[g], 0, n, 0, r), ACT.Copy)\
                        .then_inc(S(f"pts_ev{l}"), 1)
                if s + 1 < NS:
                    exps(s + 1)
                if s:
                    evac_o(s - 1)
            evac_o(NS - 1)

        def route(l):
            act.wait_ge(S(f"route_dve{l}"), upto(f"route_dve{l}", 1))
            af(sm[0], sm[0], ACT.Exp).then_inc(S(f"route_act{l}"), 1)
            act.wait_ge(S(f"route_dve{l}"), upto(f"route_dve{l}", 2))
            af(sm[4][:, 0:NT], sm[4][:, 0:NT], ACT.Exp).then_inc(S(f"route_act{l}"), 1)

        def expert(l, n, par):
            act.wait_ge(S(f"gate_mm{l}"), upto(f"gate_mm{l}", n + 1))
            if past(n):
                act.wait_ge(S(f"hid{l}"), upto(f"hid{l}", n))
            af(sil, bank(0), ACT.Silu).then_inc(S(f"silu{l}"), 1)
            act.wait_ge(S(f"hid_turned{l}"), upto(f"hid_turned{l}", n + 1))
            if past(n):
                act.wait_ge(S(f"down_mm{l}"), upto(f"down_mm{l}", n))
            af(hidt[:, :, :], g3(bank(2), 4), ACT.Copy).then_inc(S(f"hidt{l}"), 1)
            act.wait_ge(S(f"down_mm{l}"), upto(f"down_mm{l}", n + 1))
            if not (isinstance(n, int) and n < 2):
                act.wait_ge(S(f"y_rows{l}_{par}"), upto(f"y_rows{l}_{par}", n * 8 - 8 * par))
            af(yout[par][:, 0:512], bank(3), ACT.Copy).then_inc(S(f"y_a{l}"), 1)
            act.wait_ge(S(f"y_a{l}"), upto(f"y_a{l}", n + 1))
            act.wait_ge(S(f"y_v{l}"), upto(f"y_v{l}", n + 1))
            act.dma_start(y_d[bass.ds(n * CAP, CAP), :], yout[par]).then_inc(S(f"y_rows{l}_{par}"), 16)

        def experts(l):
            for n in range(2):
                expert(l, n, n)
            with act.Fori(1, NE // 2) as i:
                for par in range(2):
                    expert(l, 2 * i + par, par)

        def spilled(l):
            act.wait_ge(S(f"turns{l}"), upto(f"turns{l}", 1))
            act.wait_ge(S(f"y_rows{l}_0"), upto(f"y_rows{l}_0", 16 * NE // 2))

            def turn(n):
                act.wait_ge(S(f"general{l}_"), n * TURN + STEPS["gate_up"])
                af(sil, bank(0), ACT.Silu).then_inc(S(f"general{l}_"), 1)
                act.wait_ge(S(f"general{l}_"), n * TURN + STEPS["hid_turned"])
                af(hidt[:, :, :], g3(bank(2), 4), ACT.Copy).then_inc(S(f"general{l}_"), 1)
                act.wait_ge(S(f"general{l}_"), n * TURN + STEPS["down"])
                af(yout[0], psum[:, 2048:3072], ACT.Copy).then_inc(S(f"general{l}_"), 1)
                act.wait_ge(S(f"general{l}_"), n * TURN + STEPS["copied"])
                act.dma_start(y_d[bass.ds(n * CAP + NE * CAP, CAP), :], yout[0]).then_inc(S(f"general{l}_"), 16)

            further_rounds(act, turn)

        norm(0)
        project(0)
        act.wait_ge(S("lf_dve"), 1)
        af(lf_tmp[0], lf_tmp[0], ACT.Exp).then_inc(S("lf_act"), 1)
        act.wait_ge(S("lf_dve"), 2)
        af(lf_tmp[0], lf_tmp[0], ACT.Ln).then_inc(S("lf_act"), 1)
        for job in range(5, 15):
            turned(job)
        act.wait_ge(S("cum_mm"), 1)
        af(ckp, bank(4, 0, 512, 0, 8), ACT.Copy).then_inc(S("cum_ev"), 1)
        act.wait_ge(S("cum_mm"), 2)
        af(cks[0:64, :], psum[0:64, 0:LK], ACT.Copy).then_inc(S("cum_ev"), 1)
        act.wait_ge(S("ln_var"), 1)
        af(lnv, lnv, ACT.Sqrt).then_inc(S("ln_root"), 1)
        act.wait_ge(S("ln_done"), 1)
        for c in range(4):
            af(xt[:, c, :], xt[:, c, :], ACT.Silu, bias=lnb[:, c:c + 1], scale=lng[:, c:c + 1]).then_inc(S("a_out"), 1)
        prompt(0, HB, 4)
        samples(0, 64, 4, 4)
        norm(1)
        route(0)
        experts(0)
        spilled(0)
        norm(2)
        project(1)
        for job in range(25):
            t, kind = job // 5, job % 5
            r = rows(t)
            act.wait_ge(S("turned1"), upto("turned1", job + 1))
            cols = slice(128 * t, 128 * t + r)
            src = g3(bank(5 + job % 3), 4)[:, :, 0:r]
            if kind == 4:
                dst, src = ki[:, cols], bank(5 + job % 3, 0, r)
            else:
                dst = (qt[:, 0:4, cols], qt[:, 4:8, cols], kd[:, :, cols], qi[:, :, cols])[kind]
            af(dst, src, ACT.Copy).then_inc(S("turn_ev1"), 1)
        job = 0
        act.wait_ge(S("roped"), 5 * NT)
        for t in range(1, 4):
            for hh in range(HI):
                act.wait_ge(S("idx_mm"), job + 1)
                if job - 1 > 0:
                    act.wait_ge(S("idx_acc"), job - 1)
                n = 128 * (t + 1)
                af(relu[job % 2][:, 0:n], bank(job % 4, 0, n), ACT.Relu).then_inc(S("relu"), 1)
                job += 1
        prompt(1, HC, 0)
        samples(1, 128, 0, 8)
        norm(3)
        route(1)
        experts(1)
        spilled(1)
        for t, c0, c1 in TILES:
            h_ready(act, 4, t)
            if t > 0:
                act.wait_ge(S("sq4"), upto("sq4", t))
            af(junk[0:rows(t), :], h[0:rows(t), t, :], ACT.Square, accum_out=ssq[0:rows(t), t:t + 1])\
                .then_inc(S("sq4"), 1)
        act.wait_ge(S("ms4"), upto("ms4", 1))
        af(rstd, rstd, ACT.Sqrt).then_inc(S("root4"), 1)

    @block.vector
    def _(dve):
        v = dve
        chain = [0]

        def chained():
            chain[0] += 1
            return chain[0]

        def tt(out, x, y, op):
            return v.tensor_tensor(out, x, y, op)

        def norm(n):
            dve.wait_ge(S(f"sq{n}"), upto(f"sq{n}", NT))
            v.tensor_scalar(rstd, ssq, 1.0 / D, 1e-6, ALU.mult, ALU.add).then_inc(S(f"ms{n}"), 1)
            dve.wait_ge(S(f"root{n}"), upto(f"root{n}", 1))
            v.reciprocal(rstd, rstd).then_inc(S("dve_chain"), 1)
            dve.wait_ge(S("dve_chain"), chained())
            if n == 4:
                return
            if n == 0:
                dve.wait_ge(S("c_small"), 16)

            def evac(t):
                dve.wait_ge(S(f"hn_t{n}"), upto(f"hn_t{n}", t + 1))
                for k in range(2):
                    src = g3(bank(4 + 2 * (t % 2) + k), 4)[:, :, 0:rows(t)]
                    last = tt(xt[:, 4 * k:4 * k + 4, 128 * t:128 * t + rows(t)], src,
                              bc_last(gain[n][:, 4 * k:4 * k + 4], rows(t)), ALU.mult)
                last.then_inc(S(f"xt{n}"), 1)

            for t in range(NT):
                if t - 1 > 0:
                    dve.wait_ge(S(f"hn_t{n}"), upto(f"hn_t{n}", t - 1))
                if n % 2 and t >= 2:
                    dve.wait_ge(S(f"hn_out{n // 2}_{t % 2}"), upto(f"hn_out{n // 2}_{t % 2}", 16 * (t // 2)))
                v.tensor_scalar(hn[t % 2][0:rows(t), :], h[0:rows(t), t, :], rstd[0:rows(t), t:t + 1], None, ALU.mult)\
                    .then_inc(S(f"hn{n}"), 1)
                if t:
                    evac(t - 1)
            evac(NT - 1)

        def prompt(l, heads, chunk0, bias, beside=None):
            def scores(j):
                t = j % 4
                n = 128 * (t + 1)
                dve.wait_ge(S(f"s_mm{l}"), upto(f"s_mm{l}", j + 1))
                if j - 2 > 0:
                    dve.wait_ge(S(f"p_turned{l}"), upto(f"p_turned{l}", j - 2))
                v.tensor_tensor_reduce(sb[l][j % 3][:, 0:n], bank(S_BANK[j % 3], 0, n), bias(t), 1.0, TAKEN, ALU.add,
                                       ALU.max, mx[:, j % 3:j % 3 + 1]).then_inc(S(f"sb{l}"), 1)
                dve.wait_ge(S(f"sb{l}"), upto(f"sb{l}", j + 1))
                v.tensor_scalar(nmx[:, j % 3:j % 3 + 1], mx[:, j % 3:j % 3 + 1], -1.0, None, ALU.mult)\
                    .then_inc(S(f"nmx{l}"), 1)

            def out(hh):
                dve.wait_ge(S(f"pv{l}"), upto(f"pv{l}", hh + 1))
                p0 = 64 * (hh % 2)
                v.tensor_copy(xt[p0:p0 + 64, chunk0 + hh // 2, 0:512], bank(4 + hh % 2, 0, 512, p0, p0 + 64))\
                    .then_inc(S(f"o_ev{l}"), 1)

            scores(0)
            scores(1)
            for j in range(4 * heads):
                dve.wait_ge(S(f"exp{l}"), upto(f"exp{l}", j + 1))
                v.reciprocal(rsum[:, j % 3:j % 3 + 1], esum[:, j % 3:j % 3 + 1]).then_inc(S("dve_chain"), 1)
                dve.wait_ge(S("dve_chain"), chained())
                n = 128 * (j % 4 + 1)
                v.tensor_scalar(sb[l][j % 3][:, 0:n], sb[l][j % 3][:, 0:n], rsum[:, j % 3:j % 3 + 1], None, ALU.mult)\
                    .then_inc(S(f"probs{l}"), 1)
                if j + 2 < 4 * heads:
                    scores(j + 2)
                if beside:
                    beside(j)
                if j % 4 == 3 and j > 4:
                    out(j // 4 - 1)
            out(heads - 1)

        def largest(score, work, i):
            v.max(max8[0:score.shape[0], :], work if i else score).then_inc(S("dve_chain"), 1)
            dve.wait_ge(S("dve_chain"), chained())

        def take(score, work, keep, i):
            v.match_replace(work, max8[0:score.shape[0], :], work if i else score, TAKEN)\
                .then_inc(S("dve_chain"), 1)
            dve.wait_ge(S("dve_chain"), chained())
            if i == keep // 8 - 1:
                tt(work, work, score, ALU.is_equal).then_inc(S("dve_chain"), 1)
                dve.wait_ge(S("dve_chain"), chained())
                v.tensor_scalar(work, work, NEG, None, ALU.mult).then_inc(S("dve_chain"), 1)
                dve.wait_ge(S("dve_chain"), chained())

        def select_sample(j):
            if j % 2 == 0 and j // 2 < TOPS // 8:
                largest(score_s, sels, j // 2)
            elif j // 2 < TOPS // 8:
                take(score_s, sels, TOPS, j // 2)
                if j // 2 == TOPS // 8 - 1:
                    v.memset(tick[1], 0.0).then_inc(S("sel"), 1)

        def select_prompt(part):
            per_tile = TOPP // 8
            for i in range(3 * per_tile * part // NS, 3 * per_tile * (part + 1) // NS):
                t, k = 1 + i // per_tile, i % per_tile
                largest(score_p[t], selp[t], k)
                take(score_p[t], selp[t], TOPP, k)

        def samples(l, R):
            def top(s):
                dve.wait_ge(S(f"scored{l}"), upto(f"scored{l}", s + 1))
                v.tensor_reduce(nmx[0:R, s % 2:s % 2 + 1], psum[0:R, 0:LK], X, ALU.max, negate=True)\
                    .then_inc(S(f"nmx_s{l}"), 1)

            top(0)
            for s in range(NS):
                dve.wait_ge(S(f"exp_s{l}"), upto(f"exp_s{l}", s + 1))
                v.reciprocal(rsum[0:R, s % 2:s % 2 + 1], esum[0:R, s % 2:s % 2 + 1]).then_inc(S("dve_chain"), 1)
                dve.wait_ge(S("dve_chain"), chained())
                if s + 1 < NS:
                    top(s + 1)
                dve.wait_ge(S(f"pv_s{l}"), upto(f"pv_s{l}", s + 1))
                if l == 0:
                    if s == 0:
                        dve.wait_ge(S("headmask"), 16)
                    tt(t1[0:64, :], bank(5, 0, 512, 0, 64), headmask, ALU.mult).then_inc(S("dve_chain"), 1)
                    dve.wait_ge(S("dve_chain"), chained())
                    v.tensor_reduce(o_s[0:64, :], t1[0:64, :].rearrange("p (h d) -> p d h", h=HB), X, ALU.add)\
                        .then_inc(S("dve_chain"), 1)
                    dve.wait_ge(S("dve_chain"), chained())
                    if s > 0:
                        dve.wait_ge(S(f"o_turned{l}"), upto(f"o_turned{l}", s))
                    v.tensor_scalar(g3(o2[0:64, :], 2), bc_mid(o_s[0:64, :], 2), rsum[0:64, s % 2:s % 2 + 1], None, ALU.mult)\
                        .then_inc(S(f"osum{l}"), 1)
                else:
                    if s > 0:
                        dve.wait_ge(S(f"o_turned{l}"), upto(f"o_turned{l}", s))
                    for g in range(KVC):
                        last = v.tensor_scalar(g3(o2[32 * g:32 * g + 32, :], 2),
                                               bc_mid(bank(5, 64 * g, 64 * g + 64, 32 * g, 32 * g + 32), 2),
                                               rsum[32 * g:32 * g + 32, s % 2:s % 2 + 1], None, ALU.mult)
                    last.then_inc(S(f"osum{l}"), 1)

        def out_project(l):
            for job in range(10):
                b, t = job // 5, job % 5
                dve.wait_ge(S(f"out_mm{l}"), upto(f"out_mm{l}", job + 1))
                dst = h[0:rows(t), t, 512 * b:512 * b + 512]
                tt(dst, dst, bank(job % 4, 0, 512, 0, rows(t)), ALU.add).then_inc(S(f"out_add{l}"), 1)

        def first_max(vals, hot, tmp, top):
            v.tensor_reduce(top, vals, X, ALU.max).then_inc(S("dve_chain"), 1)
            dve.wait_ge(S("dve_chain"), chained())
            tt(tmp, vals, bc_last(top, 4), ALU.is_equal).then_inc(S("dve_chain"), 1)
            dve.wait_ge(S("dve_chain"), chained())
            tt(tmp, tmp, g3(pick4, NT), ALU.mult).then_inc(S("dve_chain"), 1)
            dve.wait_ge(S("dve_chain"), chained())
            v.tensor_reduce(sm[7][:, 0:NT], tmp, X, ALU.max).then_inc(S("dve_chain"), 1)
            dve.wait_ge(S("dve_chain"), chained())
            tt(hot, tmp, bc_last(sm[7][:, 0:NT], 4), ALU.is_equal).then_inc(S("dve_chain"), 1)
            dve.wait_ge(S("dve_chain"), chained())

        def route(l):
            for j in range(4):
                v.memset(g3(pick4, NT)[:, :, j:j + 1], 4.0 - j)
            for e in range(NE):
                v.memset(num16[:, e:e + 1], float(ROWS * e))
            v.memset(logits[:, :, :], 0.0).then_inc(S("dve_chain"), 1)
            dve.wait_ge(S("dve_chain"), chained())
            dve.wait_ge(S(f"route_mm{l}"), upto(f"route_mm{l}", 1))
            bv = bvec[:, 8 + 20 * l:28 + 20 * l]
            tt(logits[:, 0:4, :], g3(bank(2, 0, 80), 4), bc_mid(bv, 4), ALU.add)
            tt(logits[0:64, 4, :], bank(2, 80, 100, 0, 64), bv[0:64], ALU.add).then_inc(S("dve_chain"), 1)
            dve.wait_ge(S("dve_chain"), chained())
            glog, elog = logits[:, :, 0:4], logits[:, :, 4:20].rearrange("p t (g j) -> p t g j", g=NG)
            ghot, gtop = g3(sm[1], NT), sm[2][:, 0:NT]
            first_max(glog, ghot, g3(sm[3], NT), gtop)
            tt(g3(sm[0], NT), glog, bc_last(gtop, 4), ALU.subtract).then_inc(S(f"route_dve{l}"), 1)
            r4 = rtmp[0].rearrange("p (t g j) -> p t g j", t=NT, g=NG)
            tt(r4, elog, bc_last(ghot, 4), ALU.mult).then_inc(S("dve_chain"), 1)
            dve.wait_ge(S("dve_chain"), chained())
            e_in = g3(sm[5], NT)
            v.tensor_reduce(e_in, rtmp[0].rearrange("p (t g j) -> p t j g", t=NT, g=NG), X, ALU.add)\
                .then_inc(S("dve_chain"), 1)
            dve.wait_ge(S("dve_chain"), chained())
            hots = [g3(rtmp[3][:, 20 * i:20 * i + 20], NT) for i in range(2)]
            v1, v2 = rtmp[2][:, 0:NT], rtmp[2][:, 5:5 + NT]
            first_max(e_in, hots[0], g3(sm[3], NT), v1)
            v.tensor_scalar(g3(sm[6], NT), hots[0], NEG, None, ALU.mult).then_inc(S("dve_chain"), 1)
            dve.wait_ge(S("dve_chain"), chained())
            tt(e_in, e_in, g3(sm[6], NT), ALU.add).then_inc(S("dve_chain"), 1)
            dve.wait_ge(S("dve_chain"), chained())
            first_max(e_in, hots[1], g3(sm[3], NT), v2)
            tt(sm[4][:, 0:NT], v2, v1, ALU.subtract).then_inc(S(f"route_dve{l}"), 1)
            for k in range(2):
                tt(oh[k][:, :, :].rearrange("p t (g j) -> p t g j", g=NG), bc_last(ghot, 4),
                        hots[k].unsqueeze(2).broadcast_to([128, NT, NG, 4]), ALU.mult).then_inc(S("dve_chain"), 1)
                dve.wait_ge(S("dve_chain"), chained())
            v.memset(oh[0][64:128, 4, :], 0.0).then_inc(S("dve_chain"), 1)
            dve.wait_ge(S("dve_chain"), chained())
            v.memset(oh[1][64:128, 4, :], 0.0).then_inc(S("dve_chain"), 1)
            dve.wait_ge(S("dve_chain"), chained())
            tt(mask16, oh[0], oh[1], ALU.add).then_inc(S(f"mask{l}"), 1)
            dve.wait_ge(S(f"route_act{l}"), upto(f"route_act{l}", 1))
            v.tensor_reduce(sm[2][:, 0:NT], g3(sm[0], NT), X, ALU.add).then_inc(S("dve_chain"), 1)
            dve.wait_ge(S("dve_chain"), chained())
            v.reciprocal(sm[2][:, 0:NT], sm[2][:, 0:NT]).then_inc(S("dve_chain"), 1)
            dve.wait_ge(S("dve_chain"), chained())
            dve.wait_ge(S(f"route_act{l}"), upto(f"route_act{l}", 2))
            v.tensor_scalar(sm[3][:, 0:NT], sm[4][:, 0:NT], 1.0, None, ALU.add).then_inc(S("dve_chain"), 1)
            dve.wait_ge(S("dve_chain"), chained())
            v.reciprocal(sm[3][:, 0:NT], sm[3][:, 0:NT]).then_inc(S("dve_chain"), 1)
            dve.wait_ge(S("dve_chain"), chained())
            tt(wts[:, 0:NT], sm[2][:, 0:NT], sm[3][:, 0:NT], ALU.mult).then_inc(S("dve_chain"), 1)
            dve.wait_ge(S("dve_chain"), chained())
            tt(wts[:, NT:2 * NT], wts[:, 0:NT], sm[4][:, 0:NT], ALU.mult).then_inc(S("dve_chain"), 1)
            dve.wait_ge(S("dve_chain"), chained())
            dve.wait_ge(S(f"pos_mm{l}"), upto(f"pos_mm{l}", 1))
            pos = g3(bank(1, 0, NT * NE), NT)
            for k in range(2):
                rk = g3(rtmp[k], NT)
                tt(rk, pos, bc_mid(num16, NT), ALU.add).then_inc(S("dve_chain"), 1)
                dve.wait_ge(S("dve_chain"), chained())
                tt(rk, rk, oh[k], ALU.mult).then_inc(S("dve_chain"), 1)
                dve.wait_ge(S("dve_chain"), chained())
                v.tensor_reduce(rowf[:, NT * k:NT * k + NT], rk, X, ALU.add).then_inc(S("dve_chain"), 1)
                dve.wait_ge(S("dve_chain"), chained())
            v.tensor_scalar(posm, pos, 1.0, None, ALU.add).then_inc(S("dve_chain"), 1)
            dve.wait_ge(S("dve_chain"), chained())
            tt(posm, posm, mask16, ALU.mult).then_inc(S("dve_chain"), 1)
            dve.wait_ge(S("dve_chain"), chained())
            v.tensor_scalar(posm, posm, -1.0, None, ALU.add).then_inc(S("dve_chain"), 1)
            dve.wait_ge(S("dve_chain"), chained())
            for t in range(NT):
                if t - 1 > 0:
                    dve.wait_ge(S(f"tok_mm{l}"), upto(f"tok_mm{l}", t - 1))
                tt(dmat[t % 2], bc_mid(slot16, NE), bc_last(posm[:, t, :], 128), ALU.is_equal)\
                    .then_inc(S(f"dmat{l}"), 1)
            dve.wait_ge(S(f"tok_mm{l}"), upto(f"tok_mm{l}", NT))
            v.tensor_copy(tok_u, bank(3, 0, NE)).then_inc(S(f"tok{l}"), 1)
            edge, keys, got = (x[:, 0:4 * NE].rearrange("p (e r) -> p e r", r=4) for x in (rtmp[0], rtmp[1], rtmp[3]))
            for r in range(4):
                v.memset(edge[:, :, r:r + 1], float(CAP * (r + 1)))
            v.tensor_copy(sm[0][:, 0:NE], bank(2, 0, NE)).then_inc(S("dve_chain"), 1)
            dve.wait_ge(S("dve_chain"), chained())
            tt(got, bc_last(sm[0][:, 0:NE], 4), edge, ALU.is_gt)
            tt(keys, bc_last(num16, 4), edge, ALU.add).then_inc(S("dve_chain"), 1)
            dve.wait_ge(S("dve_chain"), chained())
            v.tensor_scalar(keys, keys, -1.0, LAST, ALU.mult, ALU.add).then_inc(S("dve_chain"), 1)
            dve.wait_ge(S("dve_chain"), chained())
            tt(keys, keys, got, ALU.mult).then_inc(S("dve_chain"), 1)
            dve.wait_ge(S("dve_chain"), chained())
            v.max(sm[1][:, 0:8], rtmp[1][:, 0:4 * NE]).then_inc(S("dve_chain"), 1)
            dve.wait_ge(S("dve_chain"), chained())
            v.tensor_scalar(spill_used, sm[1][0:1, 0:8], 0.0, None, ALU.is_gt).then_inc(S(f"general{l}_"), OPEN)
            v.tensor_scalar(sm[2][:, 0:8], sm[1][:, 0:8], -1.0, LAST, ALU.mult, ALU.add).then_inc(S("dve_chain"), 1)
            dve.wait_ge(S("dve_chain"), chained())
            v.tensor_copy(spill_base, sm[2][:, 0:8]).then_inc(S("dve_chain"), 1)
            dve.wait_ge(S("dve_chain"), chained())
            comp = at("WORK", 4096 + 416, 8 * NE)
            pairs = comp[0:1].rearrange("p (i e) -> p i e", i=8)
            tt(pairs, bc_last(spill_base[0:1, :], NE), bc_mid(num16[0:1], 8), ALU.is_ge).then_inc(S("dve_chain"), 1)
            dve.wait_ge(S("dve_chain"), chained())
            v.tensor_reduce(sm[3][0:1, 0:8], pairs, X, ALU.add).then_inc(S("dve_chain"), 1)
            dve.wait_ge(S("dve_chain"), chained())
            v.tensor_scalar(spill_block, sm[3][0:1, 0:8], 3.0, -3.0, ALU.mult, ALU.add).then_inc(S(f"turns{l}"), 1)
            dve.wait_ge(S(f"turns{l}"), upto(f"turns{l}", 1))
            before = comp.rearrange("p (e i) -> p e i", i=8)
            tt(before, bc_last(num16, 8), bc_mid(spill_base, NE), ALU.is_gt).then_inc(S("dve_chain"), 1)
            dve.wait_ge(S("dve_chain"), chained())
            v.tensor_reduce(sm[0][:, 0:NE], before, X, ALU.add).then_inc(S("dve_chain"), 1)
            dve.wait_ge(S("dve_chain"), chained())
            v.tensor_scalar(sm[0][:, 0:NE], sm[0][:, 0:NE], float(CAP), float(CAP * (NE - 1)), ALU.mult, ALU.add)\
                .then_inc(S("dve_chain"), 1)
            dve.wait_ge(S("dve_chain"), chained())
            v.tensor_scalar(sm[1][:, 0:NE], num16, CAP / ROWS, None, ALU.mult).then_inc(S("dve_chain"), 1)
            dve.wait_ge(S("dve_chain"), chained())
            tt(sm[0][:, 0:NE], sm[0][:, 0:NE], sm[1][:, 0:NE], ALU.subtract).then_inc(S("dve_chain"), 1)
            dve.wait_ge(S("dve_chain"), chained())
            r0, r1 = g3(rtmp[0], NT), g3(rtmp[1], NT)
            v.tensor_scalar(r0, pos, float(CAP), None, ALU.is_ge).then_inc(S("dve_chain"), 1)
            dve.wait_ge(S("dve_chain"), chained())
            tt(r0, r0, bc_mid(sm[0][:, 0:NE], NT), ALU.mult).then_inc(S("dve_chain"), 1)
            dve.wait_ge(S("dve_chain"), chained())
            tt(r0, r0, pos, ALU.add).then_inc(S("dve_chain"), 1)
            dve.wait_ge(S("dve_chain"), chained())
            tt(r0, r0, bc_mid(sm[1][:, 0:NE], NT), ALU.add).then_inc(S("dve_chain"), 1)
            dve.wait_ge(S("dve_chain"), chained())
            for k in range(2):
                tt(r1, r0, oh[k], ALU.mult).then_inc(S("dve_chain"), 1)
                dve.wait_ge(S("dve_chain"), chained())
                v.tensor_reduce(sm[3][:, NT * k:NT * k + NT], r1, X, ALU.add).then_inc(S("dve_chain"), 1)
                dve.wait_ge(S("dve_chain"), chained())
            v.tensor_copy(row_u, sm[3][:, 0:2 * NT]).then_inc(S(f"row_u{l}"), 1)

        def xgt_evac(l, n, par, done):
            for k in range(2):
                last = tt(xgt[par][:, 4 * k:4 * k + 4, :], g3(bank(6 + k), 4), bc_last(gain[2 * l + 1][:, 4 * k:4 * k + 4], 128),
                          ALU.mult)
            last.then_inc(S(done), 1)

        def expert(l, n, par, last_one=False):
            dve.wait_ge(S(f"up_mm{l}"), upto(f"up_mm{l}", n + 1))
            dve.wait_ge(S(f"silu{l}"), upto(f"silu{l}", n + 1))
            if past(n):
                dve.wait_ge(S(f"hid_turned{l}"), upto(f"hid_turned{l}", n))
            tt(hid, sil, bank(1), ALU.mult).then_inc(S(f"hid{l}"), 1)
            if not last_one:
                dve.wait_ge(S(f"xg_used{l}"), upto(f"xg_used{l}", n + 2))
                xgt_evac(l, n + 1, 1 - par, f"xgt{l}")
            dve.wait_ge(S(f"down_mm{l}"), upto(f"down_mm{l}", n + 1))
            if not (isinstance(n, int) and n < 2):
                dve.wait_ge(S(f"y_rows{l}_{par}"), upto(f"y_rows{l}_{par}", n * 8 - 8 * par))
            v.tensor_copy(yout[par][:, 512:1024], bank(4)).then_inc(S(f"y_v{l}"), 1)

        def experts(l):
            dve.wait_ge(S(f"xg_used{l}"), upto(f"xg_used{l}", 1))
            xgt_evac(l, 0, 0, f"xgt{l}")
            for n in range(2):
                expert(l, n, n)
            with dve.Fori(1, NE // 2 - 1) as i:
                for par in range(2):
                    expert(l, 2 * i + par, par)
            for n in range(NE - 2, NE):
                expert(l, n, n % 2, n == NE - 1)

        def spilled(l):

            def turn(n):
                dve.wait_ge(S(f"general{l}_"), n * TURN + OPEN)
                for k in range(2):
                    for t in range(NT):
                        last = v.tensor_scalar(places[k][:, t, :], slot16, spill_base[:, bass.ds(n, 1)],
                                               rowf[:, NT * k + t:NT * k + t + 1], ALU.add, ALU.is_equal)
                last.then_inc(S(f"general{l}_"), 1)
                dve.wait_ge(S(f"general{l}_"), n * TURN + STEPS["token_mm"])
                v.tensor_copy(idxc[0], bank(3, 0, 1)).then_inc(S(f"general{l}_"), 1)
                dve.wait_ge(S(f"general{l}_"), n * TURN + STEPS["turned"])
                xgt_evac(l, 0, 0, f"general{l}_")
                dve.wait_ge(S(f"general{l}_"), n * TURN + STEPS["silu"])
                tt(hid, sil, bank(1), ALU.mult).then_inc(S(f"general{l}_"), 1)

            dve.wait_ge(S(f"turns{l}"), upto(f"turns{l}", 1))
            further_rounds(dve, turn)

        def combine(l):
            for t in range(NT):
                hv = h[0:rows(t), t, :]
                for k in range(2):
                    i = (2 * t + k) % 4
                    dve.wait_ge(S(f"yb{l}_{i}"), upto(f"yb{l}_{i}", 16 * ((2 * t + k) // 4 + 1)))
                    ins = v.scalar_tensor_tensor(out=hv, in0=ybuf[i][0:rows(t), :],
                                                 scalar=wts[0:rows(t), NT * k + t:NT * k + t + 1], in1=hv,
                                                 op0=ALU.mult, op1=ALU.add)
                    if k == 0:
                        ins.then_inc(S("dve_chain"), 1)
                        dve.wait_ge(S("dve_chain"), chained())
                ins.then_inc(S(f"combined{l}"), 1)

        v.memset(ssq, 1.0).then_inc(S("init"), 1)
        norm(0)
        for t in range(NT):
            dve.wait_ge(S("proj_ev0"), 5 + t + 1)
            tt(A0[0:rows(t), t, 0:512], A0[0:rows(t), t, 0:512], A0[0:rows(t), t, 512:1024], ALU.mult)\
                .then_inc(S("u_ready"), 1)
        dve.wait_ge(S("turn_ev0"), 5)
        for j in range(CW):
            for c in range(4):
                op, ip = conv_p[:, c, :], ucp[:, c, j:j + SEQ]
                w = wdw[:, c, j:j + 1]
                if j == 0:
                    last = v.tensor_scalar(op, ip, w, bdw[:, c:c + 1], ALU.mult, ALU.add)
                else:
                    last = v.scalar_tensor_tensor(out=op, in0=ip, scalar=w, in1=op, op0=ALU.mult, op1=ALU.add)
            if j < CW - 1:
                last.then_inc(S("dve_chain"), 1)
                dve.wait_ge(S("dve_chain"), chained())
        last.then_inc(S("conv"), 1)
        dve.wait_ge(S("c_misc"), 16 * 6)
        dve.wait_ge(S("tail_ev0"), 2)
        x3 = [g3(lf_tmp[i], NT) for i in range(3)]
        tt(x3[1], lft, bc_mid(bvec[:, 0:8], NT), ALU.add).then_inc(S("dve_chain"), 1)
        dve.wait_ge(S("dve_chain"), chained())
        v.scalar_tensor_tensor(out=lf_tmp[0], in0=lf_tmp[1], scalar=-1.0, in1=lf_tmp[1], op0=ALU.mult, op1=ALU.min)\
            .then_inc(S("lf_dve"), 1)
        v.tensor_scalar(lf_tmp[2], lf_tmp[1], 0.0, None, ALU.min).then_inc(S("dve_chain"), 1)
        dve.wait_ge(S("dve_chain"), chained())
        dve.wait_ge(S("lf_act"), 1)
        v.tensor_scalar(lf_tmp[0], lf_tmp[0], 1.0, None, ALU.add).then_inc(S("lf_dve"), 1)
        dve.wait_ge(S("lf_act"), 2)
        tt(lft, x3[2], x3[0], ALU.subtract).then_inc(S("logf"), 1)
        dve.wait_ge(S("turn_ev0"), 15)
        v.memset(qbd_even[:, :, :, :], 0.0).then_inc(S("dve_chain"), 1)
        dve.wait_ge(S("dve_chain"), chained())
        for hh in range(HB):
            p0 = 64 * (hh % 2)
            last = v.tensor_copy(qbd_even[p0:p0 + 64, hh // 2, :, 8 * hh:8 * hh + 8],
                                 g3(qt[p0:p0 + 64, hh // 2, SEQ:TOK], NS))
        last.then_inc(S("qbd0"), 1)
        dve.wait_ge(S("fox_k_out"), 32)
        dve.wait_ge(S("ln_mm"), 1)
        tt(xt[:, 0:4, 0:SEQ], conv_p, bc_mid(bank(0), 4), ALU.subtract)
        tt(xt[:, 0:4, SEQ:TOK], conv_s, bc_mid(bank(1, 0, 64), 4), ALU.subtract)\
            .then_inc(S("dve_chain"), 1)
        dve.wait_ge(S("dve_chain"), chained())
        tt(sqv, xt[:, 0:4, :], xt[:, 0:4, :], ALU.mult).then_inc(S("squares"), 1)
        dve.wait_ge(S("ln_mm"), 2)
        v.tensor_scalar(lnv[:, 0:SEQ], bank(2), 1e-5, None, ALU.add)
        v.tensor_scalar(lnv[:, SEQ:TOK], bank(3, 0, 64), 1e-5, None, ALU.add).then_inc(S("ln_var"), 1)
        dve.wait_ge(S("ln_root"), 1)
        v.reciprocal(lnv, lnv).then_inc(S("dve_chain"), 1)
        dve.wait_ge(S("dve_chain"), chained())
        tt(xt[:, 0:4, :], xt[:, 0:4, :], bc_mid(lnv, 4), ALU.mult).then_inc(S("ln_done"), 1)
        prompt(0, HB, 4, lambda t: causal[:, 384 - 128 * t:512])
        samples(0, 64)
        out_project(0)
        norm(1)
        route(0)
        experts(0)
        spilled(0)
        combine(0)
        norm(2)
        def rotate(x, heads, t, done):
            r = rows(t)
            x4 = x.rearrange("p (h d) -> p h d", h=heads)
            x1, x2 = x4[:, :, 0:32], x4[:, :, 32:64]
            cs = bc_mid(rope[0:r, t, 0:32], heads)
            sn = bc_mid(rope[0:r, t, 32:64], heads)
            if done > 0:
                dve.wait_ge(S("roped"), done)
            a1, a2 = [g3(rot[i][0:r, 0:32 * heads], heads) for i in range(2)]
            tt(a1, x1, sn, ALU.mult)
            tt(a2, x2, sn, ALU.mult)
            tt(x1, x1, cs, ALU.mult)
            tt(x2, x2, cs, ALU.mult).then_inc(S("dve_chain"), 1)
            dve.wait_ge(S("dve_chain"), chained())
            tt(x1, x1, a2, ALU.subtract)
            tt(x2, x2, a1, ALU.add).then_inc(S("roped"), 1)

        for kind in range(3):
            for t in range(NT):
                buf, heads, last_block = ((A0[:, t, :], 16, 1), (A3[:, t, 0:256], 4, 2), (A1[:, t, :], 8, 3))[kind]
                dve.wait_ge(S("proj_ev1"), upto("proj_ev1", 5 * last_block + t + 1))
                rotate(buf[0:rows(t)], heads, t, NT * kind + t)
        dve.wait_ge(S("tail_ev1"), upto("tail_ev1", 2))
        for t in range(NT):
            r = rows(t)
            rotate(tail_odd[0:r, t, 0:64], 1, t, 3 * NT + 2 * t)
            dve.wait_ge(S("roped"), 3 * NT + 2 * t + 1)
            if 5 * (t - 1) > 0:
                dve.wait_ge(S("turned1"), upto("turned1", 5 * (t - 1)))
            v.tensor_copy(kdup[t % 2][0:r, 0:512].rearrange("p (g a d) -> p g a d", g=4, a=2),
                          g3(A3[0:r, t, 0:256], 4).unsqueeze(2).broadcast_to([r, 4, 2, 64]))
            v.tensor_copy(g3(kdup[t % 2][0:r, 512:640], 2), bc_mid(tail_odd[0:r, t, 0:64], 2))\
                .then_inc(S("roped"), 1)
        for t in range(4):
            last = v.tensor_scalar(wis[:, t, :], tail_odd[:, t, 64:72], float(HI) ** -0.5, None, ALU.mult)
        last.then_inc(S("dve_chain"), 1)
        dve.wait_ge(S("dve_chain"), chained())
        dve.wait_ge(S("turn_ev1"), upto("turn_ev1", 25))
        for hh in range(HI):
            p0 = 64 * (hh % 2)
            last = v.tensor_copy(g3(qis, NS)[:, :, 8 * hh:8 * hh + 8], g3(qi[p0:p0 + 64, hh // 2, SEQ:TOK], NS))
        last.then_inc(S("qis"), 1)
        for c in range(2):
            v.tensor_copy(k_new_odd[0:64, c, :], kd[0:64, 2 * c, SEQ:TOK])
            v.tensor_copy(k_new_odd[64:128, c, :], kd[64:128, 2 * c + 1, SEQ:TOK])
        job = 0
        for t in range(1, 4):
            n = 128 * (t + 1)
            for hh in range(HI):
                dve.wait_ge(S("relu"), job + 1)
                w = wis[:, t, hh:hh + 1]
                if hh == 0:
                    ins = v.tensor_scalar(score_p[t], relu[job % 2][:, 0:n], w, None, ALU.mult)
                else:
                    ins = v.scalar_tensor_tensor(out=score_p[t], in0=relu[job % 2][:, 0:n], scalar=w, in1=score_p[t],
                                                 op0=ALU.mult, op1=ALU.add)
                ins.then_inc(S("idx_acc"), 1)
                job += 1
                dve.wait_ge(S("idx_acc"), job)
            tt(score_p[t], score_p[t], causal[:, 384 - 128 * t:512], ALU.add).then_inc(S("dve_chain"), 1)
            dve.wait_ge(S("dve_chain"), chained())
        dve.wait_ge(S("wcol_in"), 16 * HI)
        v.tensor_scalar(wcol, wcol, float(HI) ** -0.5, None, ALU.mult).then_inc(S("dve_chain"), 1)
        dve.wait_ge(S("dve_chain"), chained())
        for s in range(NS):
            dve.wait_ge(S("idx_s_mm"), s + 1)
            if s > 0:
                dve.wait_ge(S("idx_sum"), s)
            v.tensor_scalar(rw, psum[0:64, 0:LK], 0.0, wcol[:, s:s + 1], ALU.max, ALU.mult).then_inc(S("relu_s"), 1)
            select_prompt(s)
        dve.wait_ge(S("idx_sum"), NS)
        v.tensor_copy(score_s, psum[0:64, 2048:2048 + LK]).then_inc(S("dve_chain"), 1)
        dve.wait_ge(S("dve_chain"), chained())
        tt(score_s[:, PAST:LK], score_s[:, PAST:LK], new_mask, ALU.add).then_inc(S("dve_chain"), 1)
        dve.wait_ge(S("dve_chain"), chained())
        dve.wait_ge(S("turn_ev1"), upto("turn_ev1", 25))

        dve.wait_ge(S("relu"), 24)
        v.tensor_copy(selp[0], causal[:, 384:512]).then_inc(S("dve_chain"), 1)
        dve.wait_ge(S("dve_chain"), chained())
        dve.wait_ge(S("idx_s_mm"), NS)
        v.memset(qbd_odd[:, :, :, :], 0.0).then_inc(S("dve_chain"), 1)
        dve.wait_ge(S("dve_chain"), chained())
        for hh in range(HC):
            g, p0 = hh // 4, 64 * (hh % 2)
            d0 = 64 * (g % 2)
            last = v.tensor_copy(qbd_odd[d0:d0 + 64, g // 2, :, 8 * hh:8 * hh + 8],
                                 g3(qt[p0:p0 + 64, hh // 2, SEQ:TOK], NS))
        last.then_inc(S("qbd1"), 1)
        prompt(1, HC, 0, lambda t: selp[t], select_sample)
        samples(1, 128)
        out_project(1)
        norm(3)
        route(1)
        experts(1)
        spilled(1)
        combine(1)
        norm(4)
        dve.wait_ge(S("c_fin"), 16)
        for t in range(NT):
            if t >= 2:
                dve.wait_ge(S(f"y_out{t % 2}"), 16 * (t // 2))
            v.scalar_tensor_tensor(out=yfin[t % 2][0:rows(t), :], in0=h[0:rows(t), t, :],
                                   scalar=rstd[0:rows(t), t:t + 1], in1=fin_g[0:rows(t), :], op0=ALU.mult,
                                   op1=ALU.mult).then_inc(S("y_ready"), 1)

    ctx.close()


_OUTS = [("y_prompt", (1, SEQ, D)), ("y_sample", (NS, DS, D)),
         ("conv_state_prompt", (1, 1, CW - 1, CA)), ("conv_state_sample", (1, NS, CW - 1, CA)),
         ("fox_k_prompt", (1, 1, SEQ, HB, 64)), ("fox_k_sample", (1, NS, DS, HB, 64)),
         ("fox_v_prompt", (1, 1, SEQ, HB, 64)), ("fox_v_sample", (1, NS, DS, HB, 64)),
         ("fox_logf_prompt", (1, 1, SEQ, HB)), ("fox_logf_sample", (1, NS, DS, HB)),
         ("dsa_k_prompt", (1, 1, SEQ, KVC, 64)), ("dsa_k_sample", (1, NS, DS, KVC, 64)),
         ("dsa_v_prompt", (1, 1, SEQ, KVC, 64)), ("dsa_v_sample", (1, NS, DS, KVC, 64)),
         ("dsa_kidx_prompt", (1, 1, SEQ, 64)), ("dsa_kidx_sample", (1, NS, DS, 64))]


def constants():
    f = np.float32
    p = np.arange(128)
    diag = np.where(p[None, :] <= p[:, None], 0.0, NEG).astype(f)
    causal = np.concatenate([np.zeros((128, 384), f), diag], axis=1)
    tri = np.where(np.arange(LK)[None, :] >= p[:, None], -1.0, 0.0).astype(f)
    sel = np.zeros((72, NS, HB, DS), f)
    for s in range(NS):
        for hh in range(HB):
            sel[8 * s + hh, s, hh, :] = 1.0
    for q in range(DS):
        sel[64 + q, :, :, q] = 1.0
    new_rows = np.zeros((DS, LK), f)
    for q in range(DS):
        new_rows[q, PAST + q + 1:] = NEG
    es = np.zeros((NS, DS, NS, HC, DS), f)
    for s in range(NS):
        for q in range(DS):
            es[s, q, s, :, q] = 1.0
    ohw = np.zeros((HI, DS, 120), f)
    for q in range(DS):
        ohw[:, q, 56 + q] = 1.0
    pos = np.concatenate([np.arange(SEQ), np.tile(PAST + np.arange(DS), NS), np.zeros(64)]).astype(f)
    inv = (np.float32(10000.0) ** (-np.arange(32, dtype=f) / np.float32(32))).astype(f)
    ang = (pos[:, None] * inv[None, :]).astype(f)
    rope = np.concatenate([np.cos(ang), np.sin(ang)], axis=1).astype(f).reshape(NT, 128, 64)
    misc = np.zeros((128, 390), np.float16)
    misc[:, 0:128] = p[:, None] < p[None, :]
    misc[:, 128:256] = 1.0
    misc[:, 256:384] = p[None, :]
    misc[:, 384:389] = p[:, None] + 128 * np.arange(NT)[None, :]
    head = np.repeat(np.eye(HB, dtype=f), 64, axis=1)
    return {
        "ident": np.eye(128, dtype=f), "causal": causal, "tri": tri, "selF": sel.reshape(72, -1),
        "new_rows": new_rows, "es": es.reshape(64, -1), "ohw": ohw.reshape(64, 120),
        "rope": np.ascontiguousarray(rope.transpose(1, 0, 2)).reshape(128, 320),
        "misc": misc.view(f), "mean_m": np.full((128, 128), 1.0 / CA, f),
        "headmask": np.repeat(head, DS, axis=0),
        "new_mask": np.tile(new_rows[:, PAST:], (NS, 1)),
    }


def layout(inp):
    a = {k: np.asarray(x) for k, x in inp.items()}

    def cols(w, c0, c1):
        w = w[:, c0:c1]
        return w.reshape(-1, 128, w.shape[1]).transpose(1, 0, 2).reshape(128, -1)

    def vec(x):
        return x.reshape(-1, 128).T

    even, odd = a["w_in_even"][0], a["w_in_odd"][0]
    blocks = []
    for l, (win, wout) in enumerate(((even, a["w_out_even"][0]), (odd, a["w_out_odd"][0]))):
        blocks += [cols(win, 512 * b, 512 * b + 512) for b in range(NBLK[l])]
        blocks += [cols(wout, 512 * b, 512 * b + 512) for b in range(2)]
        for e in range(NE):
            blocks += [cols(a["w_gate"][l, e], 0, FF), cols(a["w_up"][l, e], 0, FF), cols(a["w_down"][l, e], 0, D)]
    wr = [cols(np.concatenate([a["w_group"][l], a["w_router"][l]], axis=1), 0, 20) for l in range(2)]
    small = [vec(a["norm_mix_even"][0]), vec(a["norm_ffn"][0]), vec(a["norm_mix_odd"][0]), vec(a["norm_ffn"][1]),
             vec(a["b_dw"][0]), vec(a["ln_conv_g"][0]), vec(a["ln_conv_b"][0]),
             a["w_dw"][0].reshape(CW, 4, 128).transpose(2, 1, 0).reshape(128, -1)]
    bv = np.concatenate([a["b_forget"][0], a["b_group"][0], a["b_router"][0], a["b_group"][1], a["b_router"][1]])
    npool = a["cache_fox_k"].shape[1]
    out = {
        "x_prompt": a["x_prompt"][0], "x_sample": a["x_sample"].reshape(NSAMP, D),
        "state_conv": a["state_conv"][0],
        "conv_state_t": a["state_conv"][0].reshape(NS, CW - 1, 4, 128).transpose(3, 2, 0, 1),
        "fox_kt": a["cache_fox_k"][0].reshape(npool, PAGE, 4, 128).transpose(0, 3, 2, 1).reshape(npool, 128, 512),
        "fox_v": a["cache_fox_v"][0].reshape(npool, PAGE, 512),
        "logf": a["cache_fox_logf"][0],
        "dsa_page": np.concatenate([
            a["cache_dsa_k"][0].reshape(npool, PAGE, 2, 128).transpose(0, 3, 2, 1).reshape(npool, 128, 256),
            a["cache_dsa_v"][0].reshape(npool, PAGE, 256)], axis=2),
        "kidx_t": a["cache_dsa_kidx"][0].transpose(0, 2, 1),
        "page_table": a["page_table"].reshape(1, -1),
        "wstream": np.stack(blocks),
        "wtail0": cols(even, 512 * NBLK[0], 512 * NBLK[0] + TAIL[0]),
        "wtail1": cols(odd, 512 * NBLK[1], 512 * NBLK[1] + TAIL[1]),
        "wrouter": np.concatenate(wr, axis=1),
        "small": np.concatenate(small, axis=1),
        "bvec": np.broadcast_to(bv[None, :], (128, 48)),
        "fin_gain": np.broadcast_to(a["norm_final"][None, :], (128, D)),
    }
    out.update(constants())
    return {k: np.ascontiguousarray(x) for k, x in out.items()}


def kernel(**inputs):
    import concourse.bacc as bacc
    from concourse.bass_utils import run_bass_kernel_spmd

    arrays = layout(inputs)
    nc = bacc.Bacc("TRN2", target_bir_lowering=False, num_devices=1)
    a = {k: nc.dram_tensor("in_" + k, x.shape, mybir.dt.from_np(x.dtype), kind="ExternalInput").ap()
         for k, x in arrays.items()}
    o = {k: nc.dram_tensor("out_" + k, s, F32, kind="ExternalOutput").ap() for k, s in _OUTS}
    a["n_pool"] = arrays["fox_v"].shape[0]
    trunk(nc, a, o)
    r = run_bass_kernel_spmd(nc, [{"in_" + k: x for k, x in arrays.items()}], core_ids=[0])
    return tuple(r.results[0]["out_" + k] for k, _ in _OUTS)
```
